# Optimizing a Trainium2 kernel written in Bass

```python
import math
import jax, jax.numpy as jnp
from jax import lax
import numpy as np

D_MODEL = 1024
BATCH = 1
SEQ = 256
DEPTH = 2

N_A = DEPTH // 2
N_B = DEPTH - N_A

RET_HEADS = 4
RET_QK_DIM = D_MODEL // RET_HEADS
RET_V_DIM = 2 * RET_QK_DIM
RET_CHUNK = 128
RET_THETA = 10000.0
RET_IN = 2 * D_MODEL + 2 * (RET_HEADS * RET_V_DIM)

DIL_GROUPS = ((128, 1), (512, 4), (2048, 16))
N_GROUPS = len(DIL_GROUPS)
DIL_HEADS = 8
DIL_HEAD_DIM = D_MODEL // DIL_HEADS
ROT_DIMS = DIL_HEAD_DIM // 4
ROPE_THETA = 500000.0

D_FF = 4 * D_MODEL

ALPHA = (2.0 * DEPTH) ** 0.25
BETA = (8.0 * DEPTH) ** -0.25
LN_EPS = 1e-5
GN_EPS = 1e-6

kernel_name = "yoco_retention_dilated_attention_trunk"

def _layernorm(x, g, b):
    xf = x.astype(jnp.float32)
    mu = jnp.mean(xf, axis=-1, keepdims=True)
    var = jnp.mean(jnp.square(xf - mu), axis=-1, keepdims=True)
    y = (xf - mu) * lax.rsqrt(var + LN_EPS) * g.astype(jnp.float32) + b.astype(jnp.float32)
    return y.astype(x.dtype)

def _sq_relu_mlp(x, w_up, w_down):
    return jnp.square(jax.nn.relu(x @ w_up)) @ w_down

def _rotate_every_two(t):
    t1, t2 = t[..., ::2], t[..., 1::2]
    return jnp.stack((-t2, t1), axis=-1).reshape(t.shape)

def _xpos_rotation(t):
    S, dk = t.shape[1], t.shape[-1]
    angle = 1.0 / (RET_THETA ** jnp.linspace(0.0, 1.0, dk // 2, dtype=jnp.float32))
    angle = jnp.repeat(angle, 2)
    ang = jnp.arange(S, dtype=jnp.float32)[:, None] * angle[None]
    cos = jnp.cos(ang)[None, :, None, :].astype(t.dtype)
    sin = jnp.sin(ang)[None, :, None, :].astype(t.dtype)
    return t * cos + _rotate_every_two(t) * sin

def _chunkwise_retention(q, k, v):
    B, S, H, dk = q.shape
    dv = v.shape[-1]
    C = RET_CHUNK
    n = S // C
    dt = v.dtype
    log_g = jnp.log(1.0 - 2.0 ** (-5.0 - jnp.arange(H, dtype=jnp.float32)))
    idx = jnp.arange(C, dtype=jnp.float32)
    diff = idx[:, None] - idx[None, :]
    decay = jnp.where(diff[None] >= 0, jnp.exp(jnp.maximum(diff, 0.0)[None] * log_g[:, None, None]), 0.0).astype(dt)
    xi = jnp.exp((idx[None] + 1.0) * log_g[:, None]).astype(dt)
    zeta = jnp.exp((C - 1.0 - idx[None]) * log_g[:, None]).astype(dt)
    g_chunk = jnp.exp(C * log_g).astype(dt)

    def to_chunks(t):
        return t.reshape(B, n, C, H, t.shape[-1]).transpose(1, 0, 3, 2, 4)

    def step(R, inp):
        qc, kc, vc = inp
        s = jnp.einsum('bhid,bhjd->bhij', qc, kc) * decay
        o = jnp.einsum('bhij,bhjv->bhiv', s, vc) + jnp.einsum('bhid,bhdv->bhiv', qc, R) * xi[None, :, :, None]
        R = g_chunk[None, :, None, None] * R + jnp.einsum('bhjd,bhjv->bhdv', kc * zeta[None, :, :, None], vc)
        return R, o

    R0 = jnp.zeros((B, H, dk, dv), dt)
    _, o = lax.scan(step, R0, (to_chunks(q), to_chunks(k), to_chunks(v)))
    return o.transpose(1, 0, 3, 2, 4).reshape(B, S, H, dv)

def _retention_mixer(x, w_in, w_out):
    B, S, _ = x.shape
    proj = x @ w_in
    vw = RET_HEADS * RET_V_DIM
    q, k, v, g = jnp.split(proj, [D_MODEL, 2 * D_MODEL, 2 * D_MODEL + vw], axis=-1)
    q = _xpos_rotation(q.reshape(B, S, RET_HEADS, RET_QK_DIM))
    k = _xpos_rotation(k.reshape(B, S, RET_HEADS, RET_QK_DIM)) * (RET_QK_DIM ** -0.5)
    v = v.reshape(B, S, RET_HEADS, RET_V_DIM)
    o = _chunkwise_retention(q, k, v)
    of = o.astype(jnp.float32)
    of = of * lax.rsqrt(jnp.mean(jnp.square(of), axis=-1, keepdims=True) + GN_EPS)
    o = of.astype(x.dtype).reshape(B, S, vw)
    return (jax.nn.silu(g) * o) @ w_out

def _partial_rope(t):
    S = t.shape[1]
    half = ROT_DIMS // 2
    inv_freq = ROPE_THETA ** (-jnp.arange(0, ROT_DIMS, 2, dtype=jnp.float32) / ROT_DIMS)
    ang = jnp.arange(S, dtype=jnp.float32)[:, None] * inv_freq[None]
    shp = (1, S) + (1,) * (t.ndim - 3) + (half,)
    cos = jnp.cos(ang).reshape(shp).astype(t.dtype)
    sin = jnp.sin(ang).reshape(shp).astype(t.dtype)
    x1, x2, rest = t[..., :half], t[..., half:ROT_DIMS], t[..., ROT_DIMS:]
    return jnp.concatenate([x1 * cos - x2 * sin, x2 * cos + x1 * sin, rest], axis=-1)

def _shared_kv(x, kv_w):
    B, S, _ = x.shape
    kv = (x @ kv_w).reshape(B, S, 2, N_GROUPS, DIL_HEADS, DIL_HEAD_DIM)
    return _partial_rope(kv[:, :, 0]), kv[:, :, 1]

def _dilated_group(q, k, v, window, dilation):
    B, S, H, Dh = q.shape
    blk = window // dilation
    n_sub = -(-S // dilation)
    n_blk = -(-n_sub // blk)
    Lp = n_blk * blk * dilation
    pad = ((0, 0), (0, Lp - S), (0, 0), (0, 0))

    def to_blocks(t):
        return jnp.pad(t, pad).reshape(B, n_blk, blk, dilation, H, Dh)

    def with_prev(t):
        prev = jnp.pad(t, ((0, 0), (1, 0), (0, 0), (0, 0), (0, 0), (0, 0)))[:, :-1]
        return jnp.concatenate([prev, t], axis=2)

    qb = to_blocks(q)
    kc, vc = with_prev(to_blocks(k)), with_prev(to_blocks(v))
    s = jnp.einsum('bnirhd,bnjrhd->bnrhij', qb, kc).astype(jnp.float32) * (Dh ** -0.5)
    i = jnp.arange(blk)[:, None]
    j = jnp.arange(2 * blk)[None, :]
    dist = blk + i - j
    band = (dist >= 0) & (dist <= blk)
    mask = band[None] & ((jnp.arange(n_blk)[:, None, None] > 0) | (j[None] >= blk))
    s = jnp.where(mask[None, :, None, None], s, -jnp.inf)
    lse = jax.nn.logsumexp(s, axis=-1)
    p = jnp.exp(s - lse[..., None]).astype(v.dtype)
    o = jnp.einsum('bnrhij,bnjrhd->bnirhd', p, vc).reshape(B, Lp, H, Dh)[:, :S]
    lse = lse.transpose(0, 1, 4, 2, 3).reshape(B, Lp, H)[:, :S]
    return o, lse

def _dilated_mixer(x, w_q, w_out, k_sh, v_sh):
    B, S, _ = x.shape
    q = _partial_rope((x @ w_q).reshape(B, S, N_GROUPS, DIL_HEADS, DIL_HEAD_DIM))
    outs, lses = [], []
    for gi, (window, dilation) in enumerate(DIL_GROUPS):
        o, lse = _dilated_group(q[:, :, gi], k_sh[:, :, gi], v_sh[:, :, gi], window, dilation)
        outs.append(o)
        lses.append(lse)
    w = jax.nn.softmax(jnp.stack(lses, axis=0), axis=0).astype(x.dtype)
    o = jnp.sum(w[..., None] * jnp.stack(outs, axis=0), axis=0)
    return o.reshape(B, S, D_MODEL) @ w_out

def setup_inputs(seed: int = 0) -> dict:
    key = jax.random.key(seed)
    ks = jax.random.split(key, 10)

    def nrm(k, shape, fan_in, scale=1.0):
        return jax.random.normal(k, shape, jnp.float32) * (scale * fan_in ** -0.5)

    x = jax.random.normal(ks[0], (BATCH, SEQ, D_MODEL), jnp.float32)
    ret_w_in = nrm(ks[1], (N_A, D_MODEL, RET_IN), D_MODEL)
    ret_w_out = nrm(ks[2], (N_A, RET_HEADS * RET_V_DIM, D_MODEL), RET_HEADS * RET_V_DIM, BETA)
    kv_w = nrm(ks[3], (D_MODEL, 2 * N_GROUPS * D_MODEL), D_MODEL)
    dil_w_q = nrm(ks[4], (N_B, D_MODEL, N_GROUPS * D_MODEL), D_MODEL)
    dil_w_out = nrm(ks[5], (N_B, D_MODEL, D_MODEL), D_MODEL, BETA)
    mlp_w_up = nrm(ks[6], (DEPTH, D_MODEL, D_FF), D_MODEL)
    mlp_w_down = nrm(ks[7], (DEPTH, D_FF, D_MODEL), D_FF, BETA)
    ln_g = 1.0 + 0.02 * jax.random.normal(ks[8], (DEPTH, 2, D_MODEL), jnp.float32)
    ln_b = 0.02 * jax.random.normal(ks[9], (DEPTH, 2, D_MODEL), jnp.float32)
    return {"x": x, "ret_w_in": ret_w_in, "ret_w_out": ret_w_out, "kv_w": kv_w,
            "dil_w_q": dil_w_q, "dil_w_out": dil_w_out, "mlp_w_up": mlp_w_up,
            "mlp_w_down": mlp_w_down, "ln_g": ln_g, "ln_b": ln_b}

def reference(x, ret_w_in, ret_w_out, kv_w, dil_w_q, dil_w_out, mlp_w_up, mlp_w_down, ln_g, ln_b):
    k_sh, v_sh = None, None
    for l in range(DEPTH):
        if l < N_A:
            mix = _retention_mixer(x, ret_w_in[l], ret_w_out[l])
        else:
            mix = _dilated_mixer(x, dil_w_q[l - N_A], dil_w_out[l - N_A], k_sh, v_sh)
        x = _layernorm(ALPHA * x + mix, ln_g[l, 0], ln_b[l, 0])
        x = _layernorm(ALPHA * x + _sq_relu_mlp(x, mlp_w_up[l], mlp_w_down[l]), ln_g[l, 1], ln_b[l, 1])
        if l == N_A - 1:
            k_sh, v_sh = _shared_kv(x, kv_w)
    return x


_drawn_inputs = setup_inputs


def setup_inputs(seed=0):
    import zlib

    import numpy as np

    out = dict(_drawn_inputs(seed))
    spreads = {}
    factors = {}
    for name, (base, spread) in spreads.items():
        noise = np.random.default_rng([zlib.crc32(name.encode()), seed]).standard_normal(out[name].shape)
        drawn = base * np.exp(spread * noise) if base else spread * noise
        out[name] = __import__('jax').numpy.asarray(drawn.astype(out[name].dtype))
    for name, factor in factors.items():
        out[name] = (out[name] * factor).astype(out[name].dtype)
    return out
```

```python
import math
from contextlib import ExitStack

import numpy as np

import concourse.bass as bass
from concourse import mybir

F32 = mybir.dt.float32
F32R = mybir.dt.float32r
BF16 = mybir.dt.bfloat16
ALU = mybir.AluOpType
ACT = mybir.ActivationFunctionType

P = 128
D_MODEL = 1024
SEQ = 256
TILES = SEQ // P
KT = D_MODEL // P
DEPTH = 2
ALPHA = (2.0 * DEPTH) ** 0.25
LN_EPS = 1e-5
GN_EPS = 1e-6

RET_HEADS = 4
RET_QK = D_MODEL // RET_HEADS
RET_V = 2 * RET_QK
RET_HALF = RET_QK // 2

GROUPS = ((128, 1), (512, 4), (2048, 16))
NG = len(GROUPS)
HEADS = 8
HD = D_MODEL // HEADS
ROT = HD // 4
DIL_SCALE = float(HD) ** -0.5

D_FF = 4 * D_MODEL
CH = 512
FF_CHUNKS = D_FF // CH
CK = CH // P

UNIT = KT * CH
DIL_COLS = NG * HD
DIL_UNIT = KT * DIL_COLS

RET_UNITS = 4 * RET_HEADS
MLP_UNITS = 2 * FF_CHUNKS
DIL_UNITS = 3 * HEADS + 2
RET_BASE = 0
MLP_BASE = (RET_BASE + RET_UNITS, RET_BASE + RET_UNITS + MLP_UNITS + DIL_UNITS)
DIL_BASE = RET_BASE + RET_UNITS + MLP_UNITS
LAST_UNIT = MLP_BASE[1] + MLP_UNITS - 1

S0 = NG * P
S1 = NG * SEQ


class Unit:

    def __init__(self, a, b=0, i=0, size=UNIT, blocks=1):
        assert b % 2 == 0
        self.slot = a % 2
        self.number = a + b * i
        self.size = size
        self.blocks = blocks
        if blocks == NG:
            self.turn = (a - DIL_BASE) // 2 + (b // 2) * i
        else:
            self.turn = a // 2 + (b // 2) * i - (3 * HEADS // 2 if a > DIL_BASE else 0)


def stage_tables():
    f = np.float32
    pos = np.arange(SEQ, dtype=f)
    angle = (f(1.0) / (f(10000.0) ** np.linspace(0.0, 1.0, RET_HALF, dtype=f))).astype(f)
    ang = pos[:, None] * angle[None]
    ret = np.stack([np.cos(ang), np.sin(ang)], 1).astype(f)
    ret = np.concatenate([ret, ret], -1)
    ret = ret.reshape(TILES, P, 2, 2 * RET_HALF).transpose(1, 0, 2, 3)

    inv = (f(500000.0) ** (-np.arange(0, ROT, 2, dtype=f) / f(ROT))).astype(f)
    ang = pos[:, None] * inv[None]
    dil = np.stack([np.cos(ang), np.sin(ang)], 1).astype(f)
    dil = np.concatenate([dil, dil], -1)
    dil = dil.reshape(TILES, P, 2, ROT).transpose(1, 0, 2, 3)

    log_g = np.log(f(1.0) - f(2.0) ** (f(-5.0) - np.arange(RET_HEADS, dtype=f))).astype(f)
    j = np.arange(P, dtype=f)[:, None]
    i = np.arange(P, dtype=f)[None]
    decay = np.zeros((P, RET_HEADS, 3 * P), f)
    for h in range(RET_HEADS):
        inside = np.where(i >= j, np.exp(np.maximum(i - j, f(0)) * log_g[h]), f(0))
        across = np.exp((i + 1) * log_g[h]) * np.exp((P - 1 - j) * log_g[h])
        decay[:, h] = np.concatenate([inside, across, inside], 1) * f(RET_QK) ** f(-0.5)

    q = np.arange(SEQ)[:, None]
    k = np.arange(SEQ)[None]
    mask = np.zeros((P, S0 + S1), f)
    for g, (window, dilation) in enumerate(GROUPS):
        seen = (q >= k) & ((q - k) % dilation == 0) & (q - k <= window)
        m = np.where(seen, f(0), f(-1e30))
        mask[:, g * P:(g + 1) * P] = m[:P, :P]
        mask[:, S0 + g * SEQ:S0 + (g + 1) * SEQ] = m[P:]
    return {"ret_rot": ret, "dil_rot": dil, "decay": decay, "mask": mask, "ident": np.eye(P, dtype=f)}


def trunk(nc, x, ret_w_in, ret_w_out, kv_w, dil_w_q, dil_w_out, mlp_w_up, mlp_w_down, ln_g, ln_b,
          ret_rot_d, dil_rot_d, decay_d, mask_d, ident_d, out):
    with ExitStack() as ctx:
        def sb(name, shape, dt=F32):
            return ctx.enter_context(nc.sbuf_tensor(name, shape, dt))

        def sem(name):
            return ctx.enter_context(nc.semaphore(name))

        raw = sb("raw", [P, 2, UNIT])
        w_hi = sb("w_hi", [P, 2, UNIT], F32R)
        w_lo = sb("w_lo", [P, 2, UNIT], F32R)
        x_res = sb("x_res", [P, TILES, D_MODEL])
        xT_hi = sb("xT_hi", [P, KT, SEQ], F32R)
        xT_lo = sb("xT_lo", [P, KT, SEQ], F32R)
        chT_hi = sb("chT_hi", [P, CK, SEQ], F32R)
        chT_lo = sb("chT_lo", [P, CK, SEQ], F32R)
        oT_hi = sb("oT_hi", [P, HEADS, SEQ], F32R)
        oT_lo = sb("oT_lo", [P, HEADS, SEQ], F32R)
        ln_gb = sb("ln_gb", [P, 2, 2, D_MODEL])
        ret_rot = sb("ret_rot", [P, TILES, 2, 2 * RET_HALF])
        dil_rot = sb("dil_rot", [P, TILES, 2, ROT])
        decay = sb("decay", [P, RET_HEADS * 3 * P])
        mask = sb("mask", [P, S0 + S1])
        ident = sb("ident", [P, P])
        zeros = sb("zeros", [P, CH], BF16)
        stats = sb("stats", [P, TILES, 2, 6])
        moments = sb("moments", [P, TILES, 2])
        small = sb("small", [P, 32])
        neg_half = small[:, 0:1]
        var_eps = [small[:, 1 + t:2 + t] for t in range(TILES)]
        rstd = [small[:, 3 + t:4 + t] for t in range(TILES)]
        mean_sq = small[:, 5:5 + TILES]
        gn_eps_c = small[:, 21:21 + TILES]
        wait_cell = [small[:, 23 + t:24 + t] for t in range(TILES)]
        ms_eps = small[:, 7:7 + TILES]
        gn_rstd = small[:, 9:9 + TILES]
        neg_half2 = small[:, 11:11 + TILES]
        row_max = [small[:, 13 + t:14 + t] for t in range(TILES)]
        neg_max = [small[:, 15 + t:16 + t] for t in range(TILES)]
        row_sum = [small[:, 17 + t:18 + t] for t in range(TILES)]
        row_inv = [small[:, 19 + t:20 + t] for t in range(TILES)]

        arena = sb("arena", [P, 6656])
        at = [0]

        def view(cols):
            at[0] += cols
            assert at[0] <= 6656
            return arena[:, at[0] - cols:at[0]]

        def even_odd(ap):
            return ap.rearrange("p (e c) -> p e c", e=2)

        rot_c = view(2 * RET_QK)
        rot_s = view(2 * RET_QK)
        rot = view(TILES * 2 * RET_QK).rearrange("p (t e c) -> p t e c", t=TILES, e=2)
        qkT = view(2 * 2 * SEQ).rearrange("p (s e n) -> p s e n", s=2, e=2)
        v_sb = view(TILES * RET_V).rearrange("p (t c) -> p t c", t=TILES)
        silu_g = view(TILES * RET_V).rearrange("p (t c) -> p t c", t=TILES)
        sT = view(3 * P)
        gated = view(TILES * RET_V).rearrange("p (t c) -> p t c", t=TILES)
        at[0] = 0
        hid = view(TILES * CH).rearrange("p (t c) -> p t c", t=TILES)
        hid_sq = view(TILES * CH).rearrange("p (t c) -> p t c", t=TILES)
        at[0] = 0
        q_nat = view(TILES * DIL_COLS).rearrange("p (t g c) -> p t g c", t=TILES, g=NG)
        k_nat = view(TILES * DIL_COLS).rearrange("p (t g c) -> p t g c", t=TILES, g=NG)
        v_nat = view(TILES * DIL_COLS).rearrange("p (t g c) -> p t g c", t=TILES, g=NG)
        qT = view(NG * SEQ).rearrange("p (g n) -> p g n", g=NG)
        kT = view(NG * SEQ).rearrange("p (g n) -> p g n", g=NG)
        probs = view(S0 + S1)
        p0 = probs[:, 0:S0]
        p1 = probs[:, S0:]
        pT = view(NG * 3 * P).rearrange("p (g n) -> p g n", g=NG)
        dil_c = view(TILES * NG * ROT).rearrange("p (t g c) -> p t g c", t=TILES, g=NG)
        dil_s = view(TILES * NG * ROT).rearrange("p (t g c) -> p t g c", t=TILES, g=NG)

        ps_proj = ctx.enter_context(nc.psum_tensor("ps_proj", [P, TILES, CH], F32))
        ps_t = ctx.enter_context(nc.psum_tensor("ps_t", [P, 2, CH], F32))
        ps_acc = ctx.enter_context(nc.psum_tensor("ps_acc", [P, 4, CH], F32))

        def acc(t, n):
            return ps_acc[:, 2 * t + n, :]

        def dil_out(t, n):
            return ps_proj[:, t, :] if n == 0 else ps_acc[:, 1 + t, :]

        raw_landed = [[sem(f"raw_landed_{s}{f}") for f in range(2)] for s in range(2)]
        dil_landed = [sem(f"dil_landed_{s}") for s in range(2)]
        x_landed = sem("x_landed")
        ident_landed = sem("ident_landed")
        tables_landed = sem("tables_landed")
        ln_landed = [sem("ln_landed_0"), sem("ln_landed_1")]
        out_landed = sem("out_landed")
        hi_done = sem("hi_done")
        lo_done = sem("lo_done")
        tile_done = sem("tile_done")
        const_done = sem("const_done")
        xT_psum = sem("xT_psum")
        xT_hi_done = sem("xT_hi_done")
        xT_lo_done = sem("xT_lo_done")
        acc_taken = sem("acc_taken")
        ln_step = sem("ln_step")
        ln_moments = sem("ln_moments")
        ln_eps = sem("ln_eps")
        ln_rstd = sem("ln_rstd")
        x_ready = sem("x_ready")
        rot_step = sem("rot_step")
        qk_taken = sem("qk_taken")
        rot_ready = sem("rot_ready")
        qkT_psum = sem("qkT_psum")
        qT_ready = sem("qT_ready")
        kT_ready = sem("kT_ready")
        v_ready = sem("v_ready")
        g_ready = sem("g_ready")
        s_psum = sem("s_psum")
        sT_ready = sem("sT_ready")
        pv_psum = sem("pv_psum")
        squares = sem("squares")
        gn_eps = sem("gn_eps")
        gn_ready = sem("gn_ready")
        gated_ready = sem("gated_ready")
        chT_psum = sem("chT_psum")
        chT_hi_done = sem("chT_hi_done")
        chT_lo_done = sem("chT_lo_done")
        relu_ready = sem("relu_ready")
        hid_ready = sem("hid_ready")
        q_taken = sem("q_taken")
        k_taken = sem("k_taken")
        v_taken = sem("v_taken")
        rope_step = sem("rope_step")
        q_roped = sem("q_roped")
        k_roped = sem("k_roped")
        dqkT_psum = sem("dqkT_psum")
        dqT_ready = sem("dqT_ready")
        dkT_ready = sem("dkT_ready")
        scores_psum = sem("scores_psum")
        masked = sem("masked")
        max_ready = sem("max_ready")
        exp_ready = sem("exp_ready")
        inv_ready = sem("inv_ready")
        probs_ready = sem("probs_ready")
        pT_psum = sem("pT_psum")
        pT_a_ready = sem("pT_a_ready")
        pT_b_ready = sem("pT_b_ready")
        o_psum = sem("o_psum")
        oT_hi_done = sem("oT_hi_done")
        oT_lo_done = sem("oT_lo_done")

        def ret_units(h, first=False):
            if first:
                return Unit(RET_BASE, blocks=2), Unit(RET_BASE + 1), Unit(RET_BASE + 2), None
            return tuple(Unit(RET_BASE - 1 + n, 4, h, blocks=(2, 1, 1, 1)[n]) for n in range(4))

        ret_last_out = Unit(RET_BASE + RET_UNITS - 1)

        def mlp_units(m, i, first=False):
            if first:
                return Unit(MLP_BASE[m]), None
            return Unit(MLP_BASE[m] - 1, 2, i), Unit(MLP_BASE[m], 2, i)

        def mlp_last_down(m):
            return Unit(MLP_BASE[m] + MLP_UNITS - 1)

        def dil_units(pair, odd):
            return tuple(Unit(DIL_BASE + 3 * odd + n, 6, pair, DIL_UNIT, NG) for n in range(3))

        def next_dil_unit(pair, odd):
            return Unit(DIL_BASE + 3 * odd + 3, 6, pair, DIL_UNIT, NG)

        dil_out_units = [Unit(DIL_BASE + 3 * HEADS), Unit(DIL_BASE + 3 * HEADS + 1)]

        DIL_PAIRS = HEADS // 2

        block = ctx.enter_context(nc.Block())

        @block.sync
        def _(sp):
            def load(unit, source, wait=True):
                if wait:
                    sp.wait_ge(lo_done, 2 * (unit.number - 1))
                pieces = NG if unit.blocks == NG else 2
                part = unit.size // pieces
                for f in range(pieces):
                    src = source(f)
                    dst = raw[:, unit.slot, f * part:(f + 1) * part].rearrange("p (k c) -> p k c", k=src.shape[1])
                    done = dil_landed[unit.slot] if unit.blocks == NG else raw_landed[unit.slot][f]
                    sp.dma_start(dst, src).then_inc(done, 16)

            w_in = ret_w_in[0].rearrange("(k p) n -> p k n", p=P)

            def qk_cols(h):
                return lambda f: w_in[:, :, bass.ds(f * D_MODEL + h * RET_QK, RET_QK)]

            def v_cols(h):
                return lambda f: w_in[:, 4 * f:4 * f + 4, bass.ds(2 * D_MODEL + h * RET_V, RET_V)]

            def g_cols(h):
                return lambda f: w_in[:, 4 * f:4 * f + 4, bass.ds(4 * D_MODEL + h * RET_V, RET_V)]

            def out_rows(w, i):
                def rows(f):
                    r = w[bass.ds(i * CH + f * (CH // 2), CH // 2), :]
                    return r.rearrange("(k p) n -> p k n", p=P)
                return rows

            sp.dma_start(ident[:], ident_d).then_inc(ident_landed, 16)
            sp.dma_start(x_res[:], x[0].rearrange("(t p) c -> p t c", p=P)).then_inc(x_landed, 16)
            qk, v, g, _none = ret_units(0, first=True)
            load(qk, qk_cols(0), wait=False)
            load(v, v_cols(0), wait=False)
            sp.dma_start(ret_rot[:], ret_rot_d).then_inc(tables_landed, 16)
            sp.dma_start(decay[:], decay_d.rearrange("p h c -> p (h c)")).then_inc(tables_landed, 16)
            load(g, g_cols(0))

            def load_ln(layer, part):
                s = part
                sp.dma_start(ln_gb[:, s, 0, :], ln_g[layer, part:part + 1, :].partition_broadcast(P))\
                    .then_inc(ln_landed[s], 16)
                sp.dma_start(ln_gb[:, s, 1, :], ln_b[layer, part:part + 1, :].partition_broadcast(P))\
                    .then_inc(ln_landed[s], 16)

            load_ln(0, 0)
            load_ln(0, 1)
            with sp.Fori(1, RET_HEADS) as h:
                qk, v, g, o = ret_units(h)
                load(qk, qk_cols(h))
                load(v, v_cols(h))
                load(g, g_cols(h))
                load(o, out_rows(ret_w_out[0], h - 1))
            load(ret_last_out, out_rows(ret_w_out[0], RET_HEADS - 1))

            def mlp(m):
                w_up = mlp_w_up[m].rearrange("(k p) n -> p k n", p=P)

                def up_cols(i):
                    return lambda f: w_up[:, 4 * f:4 * f + 4, bass.ds(i * CH, CH)]

                up, _none = mlp_units(m, 0, first=True)
                load(up, up_cols(0))
                with sp.Fori(1, FF_CHUNKS) as i:
                    up, down = mlp_units(m, i)
                    load(up, up_cols(i))
                    load(down, out_rows(mlp_w_down[m], i - 1))
                load(mlp_last_down(m), out_rows(mlp_w_down[m], FF_CHUNKS - 1))

            mlp(0)

            sp.dma_start(dil_rot[:], dil_rot_d).then_inc(tables_landed, 16)
            sp.dma_start(mask[:], mask_d).then_inc(tables_landed, 16)
            w_q = dil_w_q[0].rearrange("(k p) n -> p k n", p=P)
            w_kv = kv_w.rearrange("(k p) n -> p k n", p=P)

            def head_cols(w, first, h):
                return lambda g: w[:, :, bass.ds((first + g) * D_MODEL + h * HD, HD)]

            def dil_pair(pair):
                for odd in range(2):
                    h = 2 * pair + odd
                    q, k, v = dil_units(pair, odd)
                    load(q, head_cols(w_q, 0, h))
                    load(k, head_cols(w_kv, 0, h))
                    load(v, head_cols(w_kv, NG, h))

            with sp.Fori(0, DIL_PAIRS) as pair:
                dil_pair(pair)
            sp.wait_ge(x_ready, 2 * TILES)
            load_ln(1, 0)
            load_ln(1, 1)
            w_o = dil_w_out[0].rearrange("(k p) n -> p k n", p=P)
            for n in range(2):
                load(dil_out_units[n], lambda f, n=n: w_o[:, 4 * f:4 * f + 4, n * CH:(n + 1) * CH])

            mlp(1)

            out_v = out[0].rearrange("(t p) c -> p t c", p=P)
            for t in range(TILES):
                sp.wait_ge(x_ready, 3 * TILES + t + 1)
                sp.dma_start(out_v[:, t, :], x_res[:, t, :]).then_inc(out_landed, 16)
            sp.wait_ge(out_landed, 16 * TILES)

        @block.gpsimd
        def _(pool):
            pool.memset(neg_half, -0.5).then_inc(const_done, 1)
            pool.memset(neg_half2, -0.5).then_inc(const_done, 1)
            pool.memset(gn_eps_c, GN_EPS).then_inc(const_done, 1)
            pool.memset(zeros[:], 0.0).then_inc(const_done, 1)
            pool.wait_ge(const_done, 3)

            def group_norm(h):
                pool.wait_ge(squares, TILES * (h + 1))
                pool.tensor_tensor(ms_eps, mean_sq, gn_eps_c, ALU.add).then_inc(gn_eps, 1)
                pool.wait_ge(gn_eps, h + 1)
                pool.tensor_tensor(gn_rstd, ms_eps, neg_half2, ALU.pow).then_inc(gn_ready, 1)

            def layer_norm(n):
                for t in range(TILES):
                    c = TILES * n + t + 1
                    pool.wait_ge(ln_moments, c)
                    pool.tensor_scalar(var_eps[t], moments[:, t, 1:2], LN_EPS, None, ALU.add).then_inc(ln_eps, 1)
                    pool.wait_ge(ln_eps, c)
                    pool.tensor_tensor(rstd[t], var_eps[t], neg_half, ALU.pow).then_inc(ln_rstd, 1)

            group_norm(0)
            with pool.Fori(1, RET_HEADS) as h:
                group_norm(h)
            for n in range(2 * DEPTH):
                layer_norm(n)

        @block.scalar
        def _(act):
            def split_hi(unit, wait=True):
                half = unit.size // 2
                for f in range(2):
                    if unit.blocks != NG:
                        act.wait_ge(raw_landed[unit.slot][f], 16 * (unit.turn + 1))
                    elif f == 0:
                        act.wait_ge(dil_landed[unit.slot], 16 * NG * (unit.turn + 1))
                    if wait and f == 0:
                        act.wait_ge(tile_done, 2 * (unit.number - 1))
                    act.activation(w_hi[:, unit.slot, f * half:(f + 1) * half],
                                   raw[:, unit.slot, f * half:(f + 1) * half], ACT.Copy).then_inc(hi_done, 1)

            def take_xT(n, t):
                act.wait_ge(xT_psum, TILES * n + t + 1)
                for b in range(2):
                    act.activation(xT_hi[:, 4 * b:4 * b + 4, t * P:(t + 1) * P],
                                   ps_t[:, b, :].rearrange("p (k c) -> p k c", k=4), ACT.Copy).then_inc(xT_hi_done, 1)

            def take_chT(n):
                act.wait_ge(chT_psum, n + 1)
                for b in range(2):
                    act.activation(chT_hi[:, 2 * b:2 * b + 2, :],
                                   ps_t[:, b, :].rearrange("p (k c) -> p k c", k=2), ACT.Copy).then_inc(chT_hi_done, 1)

            def head_squares(h):
                act.wait_ge(pv_psum, h + 1)
                for t in range(TILES):
                    act.activation(gated[:, t, :], ps_t[:, t, :], ACT.Square,
                                   scale=RET_V ** -0.5, accum_out=mean_sq[:, t:t + 1])\
                        .then_inc(squares, 1)

            def ret_head(h, first=False):
                qk, v, g, o = ret_units(h, first)
                if not first:
                    head_squares(h - 1)
                split_hi(v, wait=not first)
                if not first:
                    take_chT(h - 1)
                split_hi(g)
                for t in range(TILES):
                    act.wait_ge(tile_done, 2 * v.number + t + 1)
                    act.activation(v_sb[:, t, :], ps_proj[:, t, :], ACT.Copy).then_inc(v_ready, 1)
                act.wait_ge(qkT_psum, h + 1)
                act.activation(qkT[:, 0, :, :], ps_t[:, 0, :].rearrange("p (e n) -> p e n", e=2), ACT.Copy)\
                    .then_inc(qT_ready, 1)
                if not first:
                    split_hi(o)
                else:
                    split_hi(ret_units(1)[0])
                for t in range(TILES):
                    act.wait_ge(tile_done, 2 * g.number + t + 1)
                    act.activation(silu_g[:, t, :], ps_proj[:, t, :], ACT.Silu).then_inc(g_ready, 1)
                if not first:
                    split_hi(Unit(RET_BASE + 3, 4, h))

            split_hi(ret_units(0, first=True)[0], wait=False)
            for t in range(TILES):
                take_xT(0, t)
            ret_head(0, first=True)
            with act.Fori(1, RET_HEADS) as h:
                ret_head(h)
            head_squares(RET_HEADS - 1)
            take_chT(RET_HEADS - 1)

            def mlp(m):
                up, _none = mlp_units(m, 0, first=True)
                split_hi(up)
                for t in range(TILES):
                    take_xT(2 * m + 1, t)

                def relu(up, t):
                    act.wait_ge(tile_done, 2 * up.number + t + 1)
                    act.activation(hid[:, t, :], ps_proj[:, t, :], ACT.Relu).then_inc(relu_ready, 1)

                split_hi(mlp_units(m, 1)[0])
                for t in range(TILES):
                    relu(up, t)
                chunk0 = RET_HEADS + m * FF_CHUNKS
                with act.Fori(1, FF_CHUNKS) as i:
                    up, down = mlp_units(m, i)
                    split_hi(down)
                    take_chT(chunk0 + i - 1)
                    relu(up, 0)
                    relu(up, 1)
                    split_hi(Unit(MLP_BASE[m] + 1, 2, i))
                take_chT(chunk0 + FF_CHUNKS - 1)

            mlp(0)

            split_hi(dil_units(0, 0)[0])
            for t in range(TILES):
                take_xT(2, t)

            def copy_proj(unit, t, dst, done):
                act.wait_ge(tile_done, 2 * unit.number + t + 1)
                act.activation(dst[:, t], ps_proj[:, t, 0:DIL_COLS].rearrange("p (g c) -> p g c", g=NG), ACT.Copy)\
                    .then_inc(done, 1)

            def take_qT(p):
                act.wait_ge(dqkT_psum, p + 1)
                act.activation(qT.rearrange("p g n -> p (g n)"),
                               ps_acc[:, 0:2, :].rearrange("p b n -> p (b n)")[:, 0:NG * SEQ], ACT.Copy)\
                    .then_inc(dqT_ready, 1)

            def softmax_exp(p):
                for t, pt in ((0, p0), (1, p1)):
                    act.wait_ge(max_ready, TILES * p + t + 1)
                    act.activation(pt, pt, ACT.Exp, bias=neg_max[t], scale=DIL_SCALE, accum_out=row_sum[t])\
                        .then_inc(exp_ready, 1)

            def take_pT(p):
                act.wait_ge(pT_psum, p + 1)
                act.activation(pT[:, 0:2, :], ps_acc[:, 1:3, 0:3 * P], ACT.Copy).then_inc(pT_a_ready, 1)

            def take_oT(p):
                act.wait_ge(o_psum, p + 1)
                act.activation(oT_hi[:].rearrange("p h n -> p (h n)")[:, bass.ds(p * SEQ, SEQ)],
                               ps_acc[:, 0, 0:SEQ], ACT.Copy).then_inc(oT_hi_done, 1)

            def dil_head(pair, odd, first=False, last=False):
                h = 2 * pair + odd
                q, k, v = dil_units(pair, odd)
                if not first:
                    take_qT(h - 1)
                split_hi(k)
                copy_proj(q, 0, q_nat, q_taken)
                if not first:
                    softmax_exp(h - 1)
                copy_proj(q, 1, q_nat, q_taken)
                split_hi(v)
                if not first:
                    take_pT(h - 1)
                copy_proj(k, 0, k_nat, k_taken)
                copy_proj(k, 1, k_nat, k_taken)
                if not first:
                    take_oT(h - 1)
                if last:
                    split_hi(dil_out_units[0])
                else:
                    split_hi(next_dil_unit(pair, odd))
                copy_proj(v, 0, v_nat, v_taken)
                copy_proj(v, 1, v_nat, v_taken)

            dil_head(0, 0, first=True)
            with act.Fori(0, DIL_PAIRS - 1) as pair:
                dil_head(pair, 1)
                dil_head(pair + 1, 0)
            dil_head(DIL_PAIRS - 1, 1, last=True)
            take_qT(HEADS - 1)
            split_hi(dil_out_units[1])
            softmax_exp(HEADS - 1)
            take_pT(HEADS - 1)
            take_oT(HEADS - 1)

            mlp(1)

        @block.vector
        def _(dve):
            def split_lo(unit):
                half = unit.size // 2
                for f in range(2):
                    cols = slice(f * half, (f + 1) * half)
                    dve.wait_ge(hi_done, 2 * unit.number + f + 1)
                    dve.tensor_tensor(w_lo[:, unit.slot, cols], raw[:, unit.slot, cols],
                                      w_hi[:, unit.slot, cols].bitcast(F32), ALU.subtract).then_inc(lo_done, 1)

            def take_xT(n, t):
                for b in range(2):
                    dve.wait_ge(xT_hi_done, 2 * TILES * n + 2 * t + b + 1)
                    s = slice(t * P, (t + 1) * P)
                    dve.tensor_tensor(xT_lo[:, 4 * b:4 * b + 4, s], ps_t[:, b, :].rearrange("p (k c) -> p k c", k=4),
                                      xT_hi[:, 4 * b:4 * b + 4, s].bitcast(F32), ALU.subtract).then_inc(xT_lo_done, 1)

            def take_chT(n):
                for b in range(2):
                    dve.wait_ge(chT_hi_done, 2 * n + b + 1)
                    dve.tensor_tensor(chT_lo[:, 2 * b:2 * b + 2, :],
                                      ps_t[:, b, :].rearrange("p (k c) -> p k c", k=2),
                                      chT_hi[:, 2 * b:2 * b + 2, :].bitcast(F32), ALU.subtract)\
                        .then_inc(chT_lo_done, 1)

            steps = [0]

            def ln_chain(ins):
                steps[0] += 1
                ins.then_inc(ln_step, 1)
                dve.wait_ge(ln_step, steps[0])

            def layer_norm(n, t, last_unit, src):
                dve.wait_ge(tile_done, 2 * last_unit.number + t + 1)
                row = x_res[:, t, :]
                for c in range(2):
                    half = x_res[:, t, c * CH:(c + 1) * CH]
                    ins = dve.scalar_tensor_tensor(out=half, in0=half, scalar=ALPHA, in1=src(t, c),
                                                   op0=ALU.mult, op1=ALU.add)
                    ins.then_inc(acc_taken, 1)
                    dve.wait_ge(acc_taken, 2 * (TILES * n + t) + c + 1)
                    ln_chain(dve.bn_stats(stats[:, t, c, :], half))
                dve.bn_aggr(moments[:, t, :], stats[:, t, :, :]).then_inc(ln_moments, 1)
                dve.wait_ge(ln_moments, TILES * n + t + 1)
                dve.wait_ge(ln_landed[n % 2], 32 * (n // 2 + 1))
                ln_chain(dve.scalar_tensor_tensor(out=row, in0=row, scalar=moments[:, t, 0:1],
                                                  in1=ln_gb[:, n % 2, 0, :], op0=ALU.subtract, op1=ALU.mult))
                dve.wait_ge(ln_rstd, TILES * n + t + 1)
                dve.scalar_tensor_tensor(out=row, in0=row, scalar=rstd[t], in1=ln_gb[:, n % 2, 1, :],
                                         op0=ALU.mult, op1=ALU.add).then_inc(x_ready, 1)

            def rotate(qk, t, h):
                dve.wait_ge(tile_done, 2 * qk.number + t + 1)
                c = TILES * h + t
                pairs = ps_proj[:, t, :].rearrange("p (c e) -> p e c", e=2)
                cos = ret_rot[:, t, 0:1, :].to_broadcast([P, 2, 2 * RET_HALF])
                sin = ret_rot[:, t, 1:2, :].to_broadcast([P, 2, 2 * RET_HALF])
                mc, ms = even_odd(rot_c), even_odd(rot_s)
                dve.tensor_tensor(mc, pairs, cos, ALU.mult).then_inc(rot_step, 1)
                dve.tensor_tensor(ms, pairs, sin, ALU.mult).then_inc(qk_taken, 1)
                dve.wait_ge(rot_step, 2 * c + 1)
                dve.wait_ge(qk_taken, c + 1)
                dve.tensor_tensor(rot[:, t, 0, :], mc[:, 0], ms[:, 1], ALU.subtract).then_inc(rot_step, 1)
                dve.tensor_tensor(rot[:, t, 1, :], mc[:, 1], ms[:, 0], ALU.add).then_inc(rot_ready, 1)
                dve.wait_ge(rot_step, 2 * c + 2)
                dve.wait_ge(rot_ready, c + 1)

            def gate(h):
                dve.wait_ge(gn_ready, h + 1)
                for t in range(TILES):
                    dve.wait_ge(g_ready, TILES * h + t + 1)
                    dve.scalar_tensor_tensor(out=gated[:, t, :], in0=ps_t[:, t, :], scalar=gn_rstd[:, t:t + 1],
                                             in1=silu_g[:, t, :], op0=ALU.mult, op1=ALU.mult)\
                        .then_inc(gated_ready, 1)

            def ret_head(h, first=False):
                qk, v, g, o = ret_units(h, first)
                if not first:
                    gate(h - 1)
                split_lo(v)
                rotate(qk, 0, h)
                rotate(qk, 1, h)
                if not first:
                    take_chT(h - 1)
                split_lo(g)
                dve.wait_ge(qkT_psum, h + 1)
                dve.tensor_copy(qkT[:, 1, :, :], ps_t[:, 1, :].rearrange("p (e n) -> p e n", e=2))\
                    .then_inc(kT_ready, 1)
                split_lo(o if not first else ret_units(1)[0])
                dve.wait_ge(s_psum, h + 1)
                dve.tensor_tensor(sT, ps_t[:, 0, 0:3 * P], decay[:, bass.ds(h * 3 * P, 3 * P)], ALU.mult)\
                    .then_inc(sT_ready, 1)
                if not first:
                    split_lo(Unit(RET_BASE + 3, 4, h))

            split_lo(ret_units(0, first=True)[0])
            for t in range(TILES):
                take_xT(0, t)
            dve.wait_ge(tables_landed, 16 * 2)
            ret_head(0, first=True)
            with dve.Fori(1, RET_HEADS) as h:
                ret_head(h)
            gate(RET_HEADS - 1)
            take_chT(RET_HEADS - 1)

            def norm_and_transpose(n, last_unit, src):
                for t in range(TILES):
                    layer_norm(n, t, last_unit, src)
                    take_xT(n + 1, t)

            def mlp(m, last_unit, src):
                up, _none = mlp_units(m, 0, first=True)
                split_lo(up)
                norm_and_transpose(2 * m, last_unit, src)

                def square(t, n):
                    dve.wait_ge(relu_ready, TILES * n + t + 1)
                    dve.tensor_tensor(hid_sq[:, t, :], hid[:, t, :], hid[:, t, :], ALU.mult).then_inc(hid_ready, 1)

                n0 = m * FF_CHUNKS
                split_lo(mlp_units(m, 1)[0])
                square(0, n0)
                square(1, n0)
                with dve.Fori(1, FF_CHUNKS) as i:
                    up, down = mlp_units(m, i)
                    split_lo(down)
                    take_chT(RET_HEADS + n0 + i - 1)
                    square(0, n0 + i)
                    square(1, n0 + i)
                    split_lo(Unit(MLP_BASE[m] + 1, 2, i))
                take_chT(RET_HEADS + n0 + FF_CHUNKS - 1)

            mlp(0, ret_last_out, acc)

            split_lo(dil_units(0, 0)[0])
            norm_and_transpose(1, mlp_last_down(0), acc)
            dve.wait_ge(tables_landed, 16 * 4)

            def rope(nat, h, is_k, roped):
                n = 2 * h + is_k
                x12 = nat[:, :, :, 0:ROT]
                cos = dil_rot[:, :, 0:1, :].to_broadcast([P, TILES, NG, ROT])
                sin = dil_rot[:, :, 1:2, :].to_broadcast([P, TILES, NG, ROT])
                hr = ROT // 2
                dve.tensor_tensor(dil_c, x12, cos, ALU.mult).then_inc(rope_step, 1)
                dve.tensor_tensor(dil_s, x12, sin, ALU.mult).then_inc(rope_step, 1)
                dve.wait_ge(rope_step, 3 * n + 2)
                dve.tensor_tensor(nat[:, :, :, 0:hr], dil_c[:, :, :, 0:hr], dil_s[:, :, :, hr:ROT], ALU.subtract)\
                    .then_inc(rope_step, 1)
                dve.tensor_tensor(nat[:, :, :, hr:ROT], dil_c[:, :, :, hr:ROT], dil_s[:, :, :, 0:hr], ALU.add)\
                    .then_inc(roped, 1)
                dve.wait_ge(rope_step, 3 * n + 3)
                dve.wait_ge(roped, h + 1)

            def take_kT(p):
                dve.wait_ge(dqkT_psum, p + 1)
                dve.tensor_copy(kT.rearrange("p g n -> p (g n)"),
                                ps_acc[:, 2:4, :].rearrange("p b n -> p (b n)")[:, 0:NG * SEQ])\
                    .then_inc(dkT_ready, 1)

            def softmax_max(p):
                parts = ((0, p0, ps_acc[:, 0, 0:S0], mask[:, 0:S0]),
                         (1, p1, ps_t[:].rearrange("p b n -> p (b n)")[:, 0:S1], mask[:, S0:]))
                for t, pt, scores, m in parts:
                    dve.wait_ge(scores_psum, TILES * p + t + 1)
                    dve.memset(wait_cell[t], 0.0)
                    dve.tensor_tensor_reduce(pt, scores, m, 1.0, -3.0e38, ALU.add, ALU.max, row_max[t])\
                        .then_inc(masked, 1)
                    dve.wait_ge(masked, TILES * p + t + 1)
                    dve.tensor_scalar(neg_max[t], row_max[t], -DIL_SCALE, None, ALU.mult).then_inc(max_ready, 1)

            def softmax_norm(p):
                for t, pt in ((0, p0), (1, p1)):
                    dve.wait_ge(exp_ready, TILES * p + t + 1)
                    dve.reciprocal(row_inv[t], row_sum[t]).then_inc(inv_ready, 1)
                    dve.wait_ge(inv_ready, TILES * p + t + 1)
                    dve.tensor_scalar(pt, pt, row_inv[t], None, ALU.mult).then_inc(probs_ready, 1)

            def take_pT(p):
                dve.wait_ge(pT_psum, p + 1)
                dve.tensor_copy(pT[:, 2, :], ps_acc[:, 3, 0:3 * P]).then_inc(pT_b_ready, 1)

            def take_oT(p):
                dve.wait_ge(oT_hi_done, p + 1)
                cols = bass.ds(p * SEQ, SEQ)
                dve.tensor_tensor(oT_lo[:].rearrange("p h n -> p (h n)")[:, cols], ps_acc[:, 0, 0:SEQ],
                                  oT_hi[:].rearrange("p h n -> p (h n)")[:, cols].bitcast(F32), ALU.subtract)\
                    .then_inc(oT_lo_done, 1)

            def dil_head(pair, odd, first=False, last=False):
                h = 2 * pair + odd
                q, k, v = dil_units(pair, odd)
                if not first:
                    take_kT(h - 1)
                split_lo(k)
                if not first:
                    softmax_max(h - 1)
                    softmax_norm(h - 1)
                dve.wait_ge(q_taken, TILES * (h + 1))
                rope(q_nat, h, 0, q_roped)
                split_lo(v)
                if not first:
                    take_pT(h - 1)
                dve.wait_ge(k_taken, TILES * (h + 1))
                rope(k_nat, h, 1, k_roped)
                if not first:
                    take_oT(h - 1)
                if last:
                    split_lo(dil_out_units[0])
                else:
                    split_lo(next_dil_unit(pair, odd))

            dil_head(0, 0, first=True)
            with dve.Fori(0, DIL_PAIRS - 1) as pair:
                dil_head(pair, 1)
                dil_head(pair + 1, 0)
            dil_head(DIL_PAIRS - 1, 1, last=True)
            take_kT(HEADS - 1)
            split_lo(dil_out_units[1])
            softmax_max(HEADS - 1)
            softmax_norm(HEADS - 1)
            take_pT(HEADS - 1)
            take_oT(HEADS - 1)

            mlp(1, dil_out_units[1], dil_out)
            for t in range(TILES):
                layer_norm(2 * DEPTH - 1, t, mlp_last_down(1), acc)

        @block.tensor
        def _(pe):
            def product(dst, hi, lo, whi, wlo, start, stop):
                pe.matmul(dst, hi, whi, start=start, stop=False)
                pe.matmul(dst, hi, wlo, start=False, stop=False)
                return pe.matmul(dst, lo, whi, start=False, stop=stop)

            def open_accumulators(banks):
                for bank in banks:
                    pe.matmul(bank, zeros[:, 0:P], zeros[:], start=True, stop=False)

            def wide(unit, t, ks, xh, xl, dst, cols, wait=True, inc=True, opened=False):
                half = KT // 2

                def tile(w, k):
                    if unit.blocks == 1:
                        return w[:, unit.slot, k * cols:(k + 1) * cols]
                    blocks = w[:, unit.slot, 0:unit.size].rearrange("p (b k c) -> p k b c", b=unit.blocks, k=KT)
                    return blocks[:, k]

                for k in ks:
                    if wait and unit.blocks == 1 and k % half == 0:
                        pe.wait_ge(lo_done, 2 * unit.number + k // half + 1)
                    elif wait and k == 0:
                        pe.wait_ge(lo_done, 2 * unit.number + 2)
                    x_ = slice(t * P, (t + 1) * P)
                    last = product(dst, xh[:, k, x_], xl[:, k, x_], tile(w_hi, k), tile(w_lo, k),
                                   start=(k == 0), stop=(k == KT - 1))
                if inc:
                    last.then_inc(tile_done, 1)

            def project(unit, t, cols):
                wide(unit, t, range(KT), xT_hi, xT_lo, ps_proj[:, t, 0:cols], cols, wait=(t == 0))

            def accumulate(unit, t, stop=False):
                for k in range(CK):
                    if t == 0 and k % 2 == 0:
                        pe.wait_ge(lo_done, 2 * unit.number + k // 2 + 1)
                    for n in range(2):
                        w = slice(k * D_MODEL + n * CH, k * D_MODEL + (n + 1) * CH)
                        x_ = slice(t * P, (t + 1) * P)
                        last = product(acc(t, n), chT_hi[:, k, x_], chT_lo[:, k, x_], w_hi[:, unit.slot, w],
                                       w_lo[:, unit.slot, w], start=False, stop=(stop and k == CK - 1))
                last.then_inc(tile_done, 1)

            def transpose_x(n, t):
                for k in range(KT):
                    last = pe.transpose(ps_t[:, k // 4, (k % 4) * P:(k % 4 + 1) * P],
                                        x_res[:, t, k * P:(k + 1) * P], ident[:])
                last.then_inc(xT_psum, 1)

            def transpose_chunk(src):
                for k in range(CK):
                    for t in range(TILES):
                        c = (k % 2) * SEQ + t * P
                        last = pe.transpose(ps_t[:, k // 2, c:c + P], src[:, t, k * P:(k + 1) * P], ident[:])
                last.then_inc(chT_psum, 1)

            pe.wait_ge(const_done, 4)
            open_accumulators([acc(t, n) for t in range(TILES) for n in range(2)])
            pe.wait_ge(ident_landed, 16)
            pe.wait_ge(x_landed, 16)
            for t in range(TILES):
                if t:
                    pe.wait_ge(xT_lo_done, 2)
                transpose_x(0, t)

            def transpose_gated(h):
                pe.wait_ge(gated_ready, TILES * (h + 1))
                transpose_chunk(gated)

            def ret_head(h, first=False):
                qk, v, g, o = ret_units(h, first)
                for t in range(TILES):
                    if first:
                        pe.wait_ge(xT_lo_done, 2 * (t + 1))
                    else:
                        pe.wait_ge(g_ready, TILES * (h - 1) + t + 1)
                    project(qk, t, CH)
                if not first:
                    transpose_gated(h - 1)
                for t in range(TILES):
                    pe.wait_ge(qk_taken, TILES * h + t + 1)
                    project(v, t, CH)
                pe.wait_ge(rot_ready, TILES * (h + 1))
                if not first:
                    pe.wait_ge(chT_lo_done, 2 * h)
                for s in range(2):
                    for e in range(2):
                        for t in range(TILES):
                            last = pe.transpose(ps_t[:, s, e * SEQ + t * P:e * SEQ + (t + 1) * P],
                                                rot[:, t, e, s * RET_HALF:(s + 1) * RET_HALF], ident[:])
                last.then_inc(qkT_psum, 1)
                for t in range(TILES):
                    pe.wait_ge(v_ready, TILES * h + t + 1)
                    project(g, t, CH)
                pe.wait_ge(qT_ready, h + 1)
                pe.wait_ge(kT_ready, h + 1)
                for dst, keys, queries in ((slice(0, SEQ), slice(0, P), slice(0, SEQ)),
                                           (slice(SEQ, SEQ + P), slice(P, SEQ), slice(P, SEQ))):
                    for e in range(2):
                        last = pe.matmul(ps_t[:, 0, dst], qkT[:, 1, e, keys], qkT[:, 0, e, queries],
                                         start=(e == 0), stop=(e == 1))
                last.then_inc(s_psum, 1)
                if not first:
                    pe.wait_ge(chT_lo_done, 2 * h)
                    for t in range(TILES):
                        accumulate(o, t)
                pe.wait_ge(sT_ready, h + 1)
                pe.matmul(ps_t[:, 0, :], sT[:, 0:P], v_sb[:, 0, :], start=True, stop=True)
                pe.matmul(ps_t[:, 1, :], sT[:, P:SEQ], v_sb[:, 0, :], start=True, stop=False)
                pe.matmul(ps_t[:, 1, :], sT[:, SEQ:SEQ + P], v_sb[:, 1, :], start=False, stop=True)\
                    .then_inc(pv_psum, 1)

            ret_head(0, first=True)
            with pe.Fori(1, RET_HEADS) as h:
                ret_head(h)
            transpose_gated(RET_HEADS - 1)
            pe.wait_ge(chT_lo_done, 2 * RET_HEADS)
            for t in range(TILES):
                accumulate(ret_last_out, t, stop=True)

            def next_x(n, t):
                pe.wait_ge(x_ready, TILES * (n - 1) + t + 1)
                if t:
                    pe.wait_ge(xT_lo_done, 2 * TILES * n + 2)
                transpose_x(n, t)
                return 2 * TILES * n + 2 * (t + 1)

            def mlp(m):
                up, _none = mlp_units(m, 0, first=True)
                n = 2 * m + 1
                for t in range(TILES):
                    lo_count = next_x(n, t)
                    open_accumulators([acc(t, c) for c in range(2)])
                    pe.wait_ge(xT_lo_done, lo_count)
                    project(up, t, CH)
                n0 = m * FF_CHUNKS

                def transpose_hidden(i):
                    pe.wait_ge(hid_ready, TILES * (n0 + i + 1))
                    transpose_chunk(hid_sq)

                with pe.Fori(1, FF_CHUNKS) as i:
                    up, down = mlp_units(m, i)
                    pe.wait_ge(relu_ready, TILES * (n0 + i - 1) + 1)
                    project(up, 0, CH)
                    transpose_hidden(i - 1)
                    project(up, 1, CH)
                    pe.wait_ge(chT_lo_done, 2 * (RET_HEADS + n0 + i))
                    for t in range(TILES):
                        accumulate(down, t)
                transpose_hidden(FF_CHUNKS - 1)
                pe.wait_ge(chT_lo_done, 2 * (RET_HEADS + n0 + FF_CHUNKS))
                for t in range(TILES):
                    accumulate(mlp_last_down(m), t, stop=True)

            mlp(0)

            def transpose_qk(p):
                pe.wait_ge(q_roped, p + 1)
                pe.wait_ge(k_roped, p + 1)
                for first_bank, nat in ((0, q_nat), (2, k_nat)):
                    for g in range(NG):
                        for t in range(TILES):
                            b = TILES * g + t
                            c = (b % 4) * P
                            last = pe.transpose(ps_acc[:, first_bank + b // 4, c:c + P], nat[:, t, g, :], ident[:])
                last.then_inc(dqkT_psum, 1)

            def scores(p):
                pe.wait_ge(dqT_ready, p + 1)
                pe.wait_ge(dkT_ready, p + 1)
                for g in range(NG):
                    last = pe.matmul(ps_acc[:, 0, g * P:(g + 1) * P], qT[:, g, 0:P], kT[:, g, 0:P],
                                     start=True, stop=True)
                last.then_inc(scores_psum, 1)
                for g in range(NG):
                    c = (g % 2) * SEQ
                    last = pe.matmul(ps_t[:, g // 2, c:c + SEQ], qT[:, g, P:SEQ], kT[:, g, :],
                                     start=True, stop=True)
                last.then_inc(scores_psum, 1)

            def transpose_probs(p):
                pe.wait_ge(probs_ready, TILES * (p + 1))
                for g in range(NG):
                    parts = (p0[:, g * P:(g + 1) * P], p1[:, g * SEQ:g * SEQ + P], p1[:, g * SEQ + P:(g + 1) * SEQ])
                    for b, part in enumerate(parts):
                        last = pe.transpose(ps_acc[:, 1 + g, b * P:(b + 1) * P], part, ident[:])
                last.then_inc(pT_psum, 1)

            def values(p):
                pe.wait_ge(v_taken, TILES * (p + 1))
                pe.wait_ge(pT_a_ready, p + 1)
                pe.wait_ge(pT_b_ready, p + 1)
                for g in range(NG):
                    pe.matmul(ps_acc[:, 0, 0:SEQ], v_nat[:, 0, g, :], pT[:, g, 0:SEQ],
                              start=(g == 0), stop=False, skip_group_check=True)
                    last = pe.matmul(ps_acc[:, 0, P:SEQ], v_nat[:, 1, g, :], pT[:, g, SEQ:SEQ + P],
                                     start=False, stop=(g == NG - 1), skip_group_check=True)
                last.then_inc(o_psum, 1)

            def dil_head(pair, odd, first=False):
                h = 2 * pair + odd
                q, k, v = dil_units(pair, odd)
                if first:
                    for t in range(TILES):
                        pe.wait_ge(xT_lo_done, next_x(2, t))
                        project(q, t, DIL_COLS)
                else:
                    if not (isinstance(h, int) and h == 1):
                        pe.wait_ge(oT_lo_done, h - 1)
                    transpose_qk(h - 1)
                    pe.wait_ge(v_taken, TILES * (h - 1) + 1)
                    project(q, 0, DIL_COLS)
                    scores(h - 1)
                    pe.wait_ge(v_taken, TILES * h)
                    project(q, 1, DIL_COLS)
                pe.wait_ge(q_taken, TILES * h + 1)
                project(k, 0, DIL_COLS)
                if not first:
                    transpose_probs(h - 1)
                pe.wait_ge(q_taken, TILES * (h + 1))
                project(k, 1, DIL_COLS)
                if not first:
                    values(h - 1)
                for t in range(TILES):
                    pe.wait_ge(k_taken, TILES * h + t + 1)
                    project(v, t, DIL_COLS)

            dil_head(0, 0, first=True)
            with pe.Fori(0, DIL_PAIRS - 1) as pair:
                dil_head(pair, 1)
                dil_head(pair + 1, 0)
            dil_head(DIL_PAIRS - 1, 1)
            last_h = HEADS - 1
            pe.wait_ge(oT_lo_done, last_h)
            transpose_qk(last_h)
            pe.wait_ge(v_taken, TILES * HEADS)
            wide(dil_out_units[0], 0, range(KT - 1), oT_hi, oT_lo, dil_out(0, 0), CH, inc=False)
            scores(last_h)
            wide(dil_out_units[0], 1, range(KT - 1), oT_hi, oT_lo, dil_out(1, 0), CH, wait=False, inc=False)
            transpose_probs(last_h)
            values(last_h)
            pe.wait_ge(oT_lo_done, HEADS)
            for t in range(TILES):
                wide(dil_out_units[0], t, [KT - 1], oT_hi, oT_lo, dil_out(t, 0), CH, wait=False)
            for t in range(TILES):
                wide(dil_out_units[1], t, range(KT), oT_hi, oT_lo, dil_out(t, 1), CH, wait=(t == 0))

            mlp(1)


_INS = ["x", "ret_w_in", "ret_w_out", "kv_w", "dil_w_q", "dil_w_out", "mlp_w_up", "mlp_w_down", "ln_g", "ln_b"]


def kernel(**inputs):
    import concourse.bacc as bacc
    from concourse.bass_utils import run_bass_kernel_spmd

    nc = bacc.Bacc("TRN2", target_bir_lowering=False, num_devices=1)
    arrays = {name: np.ascontiguousarray(inputs[name]) for name in _INS}
    arrays.update({name: np.ascontiguousarray(a) for name, a in stage_tables().items()})
    args = [nc.dram_tensor(f"in_{name}", a.shape, F32, kind="ExternalInput").ap() for name, a in arrays.items()]
    out = nc.dram_tensor("out", (1, SEQ, D_MODEL), F32, kind="ExternalOutput").ap()
    trunk(nc, *args, out)
    r = run_bass_kernel_spmd(nc, [{f"in_{name}": a for name, a in arrays.items()}], core_ids=[0])
    return r.results[0]["out"]
```

```python
import math
from contextlib import ExitStack

import numpy as np

import concourse.bass as bass
from concourse import mybir

F32 = mybir.dt.float32
F32R = mybir.dt.float32r
BF16 = mybir.dt.bfloat16
ALU = mybir.AluOpType
ACT = mybir.ActivationFunctionType

P = 128
D_MODEL = 1024
SEQ = 256
TILES = SEQ // P
KT = D_MODEL // P
DEPTH = 2
ALPHA = (2.0 * DEPTH) ** 0.25
LN_EPS = 1e-5
GN_EPS = 1e-6

RET_HEADS = 4
RET_QK = D_MODEL // RET_HEADS
RET_V = 2 * RET_QK
RET_HALF = RET_QK // 2

GROUPS = ((128, 1), (512, 4), (2048, 16))
NG = len(GROUPS)
HEADS = 8
HD = D_MODEL // HEADS
ROT = HD // 4
DIL_SCALE = float(HD) ** -0.5

D_FF = 4 * D_MODEL
CH = 512
FF_CHUNKS = D_FF // CH
CK = CH // P

UNIT = KT * CH
DIL_COLS = NG * HD
DIL_UNIT = KT * DIL_COLS

RET_UNITS = 4 * RET_HEADS
MLP_UNITS = 2 * FF_CHUNKS
DIL_UNITS = 3 * HEADS + 2
RET_BASE = 0
MLP_BASE = (RET_BASE + RET_UNITS, RET_BASE + RET_UNITS + MLP_UNITS + DIL_UNITS)
DIL_BASE = RET_BASE + RET_UNITS + MLP_UNITS
LAST_UNIT = MLP_BASE[1] + MLP_UNITS - 1

S0 = NG * P
S1 = NG * SEQ


class Unit:

    def __init__(self, a, b=0, i=0, size=UNIT, blocks=1):
        assert b % 2 == 0
        self.slot = a % 2
        self.number = a + b * i
        self.size = size
        self.blocks = blocks
        if blocks == NG:
            self.turn = (a - DIL_BASE) // 2 + (b // 2) * i
        else:
            self.turn = a // 2 + (b // 2) * i - (3 * HEADS // 2 if a > DIL_BASE else 0) - (a % 2 == 0)


def stage_tables():
    f = np.float32
    pos = np.arange(SEQ, dtype=f)
    angle = (f(1.0) / (f(10000.0) ** np.linspace(0.0, 1.0, RET_HALF, dtype=f))).astype(f)
    ang = pos[:, None] * angle[None]
    ret = np.stack([np.cos(ang), np.sin(ang)], 1).astype(f)
    ret = np.concatenate([ret, ret], -1)
    ret = ret.reshape(TILES, P, 2, 2 * RET_HALF).transpose(1, 0, 2, 3)

    inv = (f(500000.0) ** (-np.arange(0, ROT, 2, dtype=f) / f(ROT))).astype(f)
    ang = pos[:, None] * inv[None]
    dil = np.stack([np.cos(ang), np.sin(ang)], 1).astype(f)
    dil = np.concatenate([dil, dil], -1)
    dil = dil.reshape(TILES, P, 2, ROT).transpose(1, 0, 2, 3)

    log_g = np.log(f(1.0) - f(2.0) ** (f(-5.0) - np.arange(RET_HEADS, dtype=f))).astype(f)
    j = np.arange(P, dtype=f)[:, None]
    i = np.arange(P, dtype=f)[None]
    decay = np.zeros((P, RET_HEADS, 3 * P), f)
    for h in range(RET_HEADS):
        inside = np.where(i >= j, np.exp(np.maximum(i - j, f(0)) * log_g[h]), f(0))
        across = np.exp((i + 1) * log_g[h]) * np.exp((P - 1 - j) * log_g[h])
        decay[:, h] = np.concatenate([inside, across, inside], 1) * f(RET_QK) ** f(-0.5)

    q = np.arange(SEQ)[:, None]
    k = np.arange(SEQ)[None]
    mask = np.zeros((P, S0 + S1), f)
    for g, (window, dilation) in enumerate(GROUPS):
        seen = (q >= k) & ((q - k) % dilation == 0) & (q - k <= window)
        m = np.where(seen, f(0), f(-1e30))
        mask[:, g * P:(g + 1) * P] = m[:P, :P]
        mask[:, S0 + g * SEQ:S0 + (g + 1) * SEQ] = m[P:]
    return {"ret_rot": ret, "dil_rot": dil, "decay": decay, "mask": mask, "ident": np.eye(P, dtype=f)}


def trunk(nc, x, ret_w_in, ret_w_out, kv_w, dil_w_q, dil_w_out, mlp_w_up, mlp_w_down, ln_g, ln_b,
          ret_rot_d, dil_rot_d, decay_d, mask_d, ident_d, out):
    with ExitStack() as ctx:
        def sb(name, shape, dt=F32):
            return ctx.enter_context(nc.sbuf_tensor(name, shape, dt))

        def sem(name):
            return ctx.enter_context(nc.semaphore(name))

        raw = sb("raw", [P, 2, UNIT])
        w_hi = sb("w_hi", [P, 2, UNIT], F32R)
        w_lo = sb("w_lo", [P, 2, UNIT], F32R)
        x_res = sb("x_res", [P, TILES, D_MODEL])
        xT_hi = sb("xT_hi", [P, KT, SEQ], F32R)
        xT_lo = sb("xT_lo", [P, KT, SEQ], F32R)
        oT_hi = sb("oT_hi", [P, HEADS, SEQ], F32R)
        oT_lo = sb("oT_lo", [P, HEADS, SEQ], F32R)
        ln_gb = sb("ln_gb", [P, 2, 2, D_MODEL])
        ret_rot = sb("ret_rot", [P, TILES, 2, 2 * RET_HALF])
        dil_rot = sb("dil_rot", [P, TILES, 2, ROT])
        decay = sb("decay", [P, RET_HEADS * 3 * P])
        mask = sb("mask", [P, S0 + S1])
        ident = sb("ident", [P, P])
        zeros = sb("zeros", [P, CH], BF16)
        stats = sb("stats", [P, TILES, 2, 6])
        moments = sb("moments", [P, TILES, 2])
        small = sb("small", [P, 32])
        neg_half = small[:, 0:1]
        var_eps = [small[:, 1 + t:2 + t] for t in range(TILES)]
        rstd = [small[:, 3 + t:4 + t] for t in range(TILES)]
        mean_sq = small[:, 5:5 + TILES]
        gn_eps_c = small[:, 21:21 + TILES]
        wait_cell = [small[:, 23 + t:24 + t] for t in range(TILES)]
        ms_eps = small[:, 7:7 + TILES]
        gn_rstd = small[:, 9:9 + TILES]
        neg_half2 = small[:, 11:11 + TILES]
        row_max = [small[:, 13 + t:14 + t] for t in range(TILES)]
        neg_max = [small[:, 15 + t:16 + t] for t in range(TILES)]
        row_sum = [small[:, 17 + t:18 + t] for t in range(TILES)]
        row_inv = [small[:, 19 + t:20 + t] for t in range(TILES)]

        arena = sb("arena", [P, 6656])
        at = [0]

        def view(cols):
            at[0] += cols
            assert at[0] <= 6656
            return arena[:, at[0] - cols:at[0]]

        def even_odd(ap):
            return ap.rearrange("p (e c) -> p e c", e=2)

        rot_c = view(2 * RET_QK)
        rot_s = view(2 * RET_QK)
        rot = view(TILES * 2 * RET_QK).rearrange("p (t e c) -> p t e c", t=TILES, e=2)
        qkT = view(2 * 2 * SEQ).rearrange("p (s e n) -> p s e n", s=2, e=2)
        v_sb = view(TILES * RET_V).rearrange("p (t c) -> p t c", t=TILES)
        silu_g = view(TILES * RET_V).rearrange("p (t c) -> p t c", t=TILES)
        sT = view(3 * P)
        gated = view(TILES * RET_V).rearrange("p (t c) -> p t c", t=TILES)
        at[0] = 0
        hid = view(TILES * CH).rearrange("p (t c) -> p t c", t=TILES)
        hid_sq = view(TILES * CH).rearrange("p (t c) -> p t c", t=TILES)
        at[0] = 0
        q_nat = view(TILES * DIL_COLS).rearrange("p (t g c) -> p t g c", t=TILES, g=NG)
        k_nat = view(TILES * DIL_COLS).rearrange("p (t g c) -> p t g c", t=TILES, g=NG)
        v_nat = view(TILES * DIL_COLS).rearrange("p (t g c) -> p t g c", t=TILES, g=NG)
        qT = view(NG * SEQ).rearrange("p (g n) -> p g n", g=NG)
        kT = view(NG * SEQ).rearrange("p (g n) -> p g n", g=NG)
        probs = view(S0 + S1)
        p0 = probs[:, 0:S0]
        p1 = probs[:, S0:]
        pT = view(NG * 3 * P).rearrange("p (g n) -> p g n", g=NG)
        dil_c = view(TILES * NG * ROT).rearrange("p (t g c) -> p t g c", t=TILES, g=NG)
        dil_s = view(TILES * NG * ROT).rearrange("p (t g c) -> p t g c", t=TILES, g=NG)

        ps_proj = ctx.enter_context(nc.psum_tensor("ps_proj", [P, TILES, CH], F32))
        ps_t = ctx.enter_context(nc.psum_tensor("ps_t", [P, 2, CH], F32))
        ps_acc = ctx.enter_context(nc.psum_tensor("ps_acc", [P, 4, CH], F32))

        def acc(t, n):
            return ps_acc[:, 2 * t + n, :]

        def dil_out(t, n):
            return ps_proj[:, t, :] if n == 0 else ps_acc[:, 1 + t, :]

        raw_landed = [[sem(f"raw_landed_{s}{f}") for f in range(2)] for s in range(2)]
        first_landed = [sem(f"first_landed_{f}") for f in range(4)]
        dil_landed = [sem(f"dil_landed_{s}") for s in range(2)]
        x_landed = [sem(f"x_landed_{t}") for t in range(TILES)]
        ident_landed = sem("ident_landed")
        tables_landed = sem("tables_landed")
        ln_landed = [sem("ln_landed_0"), sem("ln_landed_1")]
        out_landed = sem("out_landed")
        first_hi = sem("first_hi")
        first_lo = sem("first_lo")
        hi_done = sem("hi_done")
        lo_done = sem("lo_done")
        tile_done = sem("tile_done")
        const_done = sem("const_done")
        xT_psum = sem("xT_psum")
        xT_hi_done = sem("xT_hi_done")
        xT_lo_done = sem("xT_lo_done")
        acc_half = sem("acc_half")
        acc_taken = sem("acc_taken")
        ln_step = sem("ln_step")
        ln_moments = sem("ln_moments")
        ln_eps = sem("ln_eps")
        ln_rstd = sem("ln_rstd")
        x_ready = sem("x_ready")
        rot_step = sem("rot_step")
        qk_taken = sem("qk_taken")
        rot_ready = sem("rot_ready")
        qkT_psum = sem("qkT_psum")
        qT_ready = sem("qT_ready")
        kT_ready = sem("kT_ready")
        v_ready = sem("v_ready")
        g_ready = sem("g_ready")
        s_psum = sem("s_psum")
        sT_ready = sem("sT_ready")
        pv_psum = sem("pv_psum")
        squares = sem("squares")
        gn_eps = sem("gn_eps")
        gn_ready = sem("gn_ready")
        gated_ready = sem("gated_ready")
        chT_psum = sem("chT_psum")
        chT_hi_done = sem("chT_hi_done")
        chT_lo_done = sem("chT_lo_done")
        relu_ready = sem("relu_ready")
        hid_ready = sem("hid_ready")
        q_taken = sem("q_taken")
        k_taken = sem("k_taken")
        v_taken = sem("v_taken")
        rope_step = sem("rope_step")
        q_roped = sem("q_roped")
        k_roped = sem("k_roped")
        dqkT_psum = sem("dqkT_psum")
        dqT_ready = sem("dqT_ready")
        dkT_ready = sem("dkT_ready")
        scores_psum = sem("scores_psum")
        masked = sem("masked")
        max_ready = sem("max_ready")
        exp_ready = sem("exp_ready")
        inv_ready = sem("inv_ready")
        probs_ready = sem("probs_ready")
        pT_psum = sem("pT_psum")
        pT_a_ready = sem("pT_a_ready")
        pT_b_ready = sem("pT_b_ready")
        o_psum = sem("o_psum")
        oT_hi_done = sem("oT_hi_done")
        oT_lo_done = sem("oT_lo_done")

        def ret_units(h, first=False):
            if first:
                return Unit(RET_BASE + 1, blocks=2), Unit(RET_BASE), Unit(RET_BASE + 2), None
            return tuple(Unit(RET_BASE - 1 + n, 4, h, blocks=(2, 1, 1, 1)[n]) for n in range(4))

        ret_last_out = Unit(RET_BASE + RET_UNITS - 1)

        def mlp_units(m, i, first=False):
            if first:
                return Unit(MLP_BASE[m]), None
            return Unit(MLP_BASE[m] - 1, 2, i), Unit(MLP_BASE[m], 2, i)

        def mlp_last_down(m):
            return Unit(MLP_BASE[m] + MLP_UNITS - 1)

        def dil_units(pair, odd):
            return tuple(Unit(DIL_BASE + 3 * odd + n, 6, pair, DIL_UNIT, NG) for n in range(3))

        def next_dil_unit(pair, odd):
            return Unit(DIL_BASE + 3 * odd + 3, 6, pair, DIL_UNIT, NG)

        dil_out_units = [Unit(DIL_BASE + 3 * HEADS), Unit(DIL_BASE + 3 * HEADS + 1)]

        DIL_PAIRS = HEADS // 2

        block = ctx.enter_context(nc.Block())

        @block.sync
        def _(sp):
            def load(unit, source, wait=True):
                if wait:
                    sp.wait_ge(lo_done, 2 * (unit.number - 1))
                pieces = NG if unit.blocks == NG else 2
                part = unit.size // pieces
                for f in range(pieces):
                    src = source(f)
                    dst = raw[:, unit.slot, f * part:(f + 1) * part].rearrange("p (k c) -> p k c", k=src.shape[1])
                    done = dil_landed[unit.slot] if unit.blocks == NG else raw_landed[unit.slot][f]
                    sp.dma_start(dst, src).then_inc(done, 16)

            w_in = ret_w_in[0].rearrange("(k p) n -> p k n", p=P)

            def qk_cols(h):
                return lambda f: w_in[:, :, bass.ds(f * D_MODEL + h * RET_QK, RET_QK)]

            def v_cols(h):
                return lambda f: w_in[:, 4 * f:4 * f + 4, bass.ds(2 * D_MODEL + h * RET_V, RET_V)]

            def g_cols(h):
                return lambda f: w_in[:, 4 * f:4 * f + 4, bass.ds(4 * D_MODEL + h * RET_V, RET_V)]

            def out_rows(w, i):
                def rows(f):
                    r = w[bass.ds(i * CH + f * (CH // 2), CH // 2), :]
                    return r.rearrange("(k p) n -> p k n", p=P)
                return rows

            sp.dma_start(ident[:], ident_d).then_inc(ident_landed, 16)
            x_v = x[0].rearrange("(t p) c -> p t c", p=P)
            for t in range(TILES):
                sp.dma_start(x_res[:, t, :], x_v[:, t, :]).then_inc(x_landed[t], 16)
            qk, v, g, _none = ret_units(0, first=True)
            for f in range(4):
                sp.dma_start(raw[:, v.slot, f * (UNIT // 4):(f + 1) * (UNIT // 4)].rearrange("p (k c) -> p k c", k=2),
                             w_in[:, 2 * f:2 * f + 2, 2 * D_MODEL:2 * D_MODEL + RET_V]).then_inc(first_landed[f], 16)
            load(qk, qk_cols(0), wait=False)
            sp.dma_start(ret_rot[:], ret_rot_d).then_inc(tables_landed, 16)
            sp.dma_start(decay[:], decay_d.rearrange("p h c -> p (h c)")).then_inc(tables_landed, 16)
            load(g, g_cols(0))

            def load_ln(layer, part):
                s = part
                sp.dma_start(ln_gb[:, s, 0, :], ln_g[layer, part:part + 1, :].partition_broadcast(P))\
                    .then_inc(ln_landed[s], 16)
                sp.dma_start(ln_gb[:, s, 1, :], ln_b[layer, part:part + 1, :].partition_broadcast(P))\
                    .then_inc(ln_landed[s], 16)

            load_ln(0, 0)
            load_ln(0, 1)
            with sp.Fori(1, RET_HEADS) as h:
                qk, v, g, o = ret_units(h)
                load(qk, qk_cols(h))
                load(v, v_cols(h))
                load(g, g_cols(h))
                load(o, out_rows(ret_w_out[0], h - 1))
            load(ret_last_out, out_rows(ret_w_out[0], RET_HEADS - 1))

            def mlp(m):
                w_up = mlp_w_up[m].rearrange("(k p) n -> p k n", p=P)

                def up_cols(i):
                    return lambda f: w_up[:, 4 * f:4 * f + 4, bass.ds(i * CH, CH)]

                up, _none = mlp_units(m, 0, first=True)
                load(up, up_cols(0))
                with sp.Fori(1, FF_CHUNKS) as i:
                    up, down = mlp_units(m, i)
                    load(up, up_cols(i))
                    load(down, out_rows(mlp_w_down[m], i - 1))
                load(mlp_last_down(m), out_rows(mlp_w_down[m], FF_CHUNKS - 1))

            mlp(0)

            sp.dma_start(dil_rot[:], dil_rot_d).then_inc(tables_landed, 16)
            sp.dma_start(mask[:], mask_d).then_inc(tables_landed, 16)
            w_q = dil_w_q[0].rearrange("(k p) n -> p k n", p=P)
            w_kv = kv_w.rearrange("(k p) n -> p k n", p=P)

            def head_cols(w, first, h):
                return lambda g: w[:, :, bass.ds((first + g) * D_MODEL + h * HD, HD)]

            def dil_pair(pair):
                for odd in range(2):
                    h = 2 * pair + odd
                    q, k, v = dil_units(pair, odd)
                    load(q, head_cols(w_q, 0, h))
                    load(k, head_cols(w_kv, 0, h))
                    load(v, head_cols(w_kv, NG, h))

            with sp.Fori(0, DIL_PAIRS) as pair:
                dil_pair(pair)
            sp.wait_ge(x_ready, 2 * 2 * TILES)
            load_ln(1, 0)
            load_ln(1, 1)
            w_o = dil_w_out[0].rearrange("(k p) n -> p k n", p=P)
            for n in range(2):
                load(dil_out_units[n], lambda f, n=n: w_o[:, 4 * f:4 * f + 4, n * CH:(n + 1) * CH])

            mlp(1)

            out_v = out[0].rearrange("(t p) c -> p t c", p=P)
            for t in range(TILES):
                for c in range(2):
                    cols = slice(c * CH, (c + 1) * CH)
                    sp.wait_ge(x_ready, 2 * (3 * TILES + t) + c + 1)
                    sp.dma_start(out_v[:, t, cols], x_res[:, t, cols]).then_inc(out_landed, 16)
            sp.wait_ge(out_landed, 16 * 2 * TILES)

        @block.gpsimd
        def _(pool):
            pool.memset(neg_half, -0.5).then_inc(const_done, 1)
            pool.memset(neg_half2, -0.5).then_inc(const_done, 1)
            pool.memset(gn_eps_c, GN_EPS).then_inc(const_done, 1)
            pool.memset(zeros[:], 0.0).then_inc(const_done, 1)
            pool.wait_ge(const_done, 3)

            def group_norm(h):
                pool.wait_ge(squares, TILES * (h + 1))
                pool.tensor_tensor(ms_eps, mean_sq, gn_eps_c, ALU.add).then_inc(gn_eps, 1)
                pool.wait_ge(gn_eps, h + 1)
                pool.tensor_tensor(gn_rstd, ms_eps, neg_half2, ALU.pow).then_inc(gn_ready, 1)

            def layer_norm(n):
                for t in range(TILES):
                    c = TILES * n + t + 1
                    pool.wait_ge(ln_moments, c)
                    pool.tensor_scalar(var_eps[t], moments[:, t, 1:2], LN_EPS, None, ALU.add).then_inc(ln_eps, 1)
                    pool.wait_ge(ln_eps, c)
                    pool.tensor_tensor(rstd[t], var_eps[t], neg_half, ALU.pow).then_inc(ln_rstd, 1)

            group_norm(0)
            with pool.Fori(1, RET_HEADS) as h:
                group_norm(h)
            for n in range(2 * DEPTH):
                layer_norm(n)

        @block.scalar
        def _(act):
            def split_hi(unit, wait=True):
                half = unit.size // 2
                for f in range(2):
                    if unit.blocks != NG:
                        act.wait_ge(raw_landed[unit.slot][f], 16 * (unit.turn + 1))
                    elif f == 0:
                        act.wait_ge(dil_landed[unit.slot], 16 * NG * (unit.turn + 1))
                    if wait and f == 0:
                        act.wait_ge(tile_done, 2 * (unit.number - 1))
                    act.activation(w_hi[:, unit.slot, f * half:(f + 1) * half],
                                   raw[:, unit.slot, f * half:(f + 1) * half], ACT.Copy).then_inc(hi_done, 1)

            def take_xT(n, t):
                for b in range(2):
                    act.wait_ge(xT_psum, 2 * (TILES * n + t) + b + 1)
                    act.activation(xT_hi[:, 4 * b:4 * b + 4, t * P:(t + 1) * P],
                                   ps_t[:, b, :].rearrange("p (k c) -> p k c", k=4), ACT.Copy).then_inc(xT_hi_done, 1)

            def take_chT(n, place=0):
                for b in range(2):
                    act.wait_ge(chT_psum, 2 * n + b + 1)
                    act.activation(oT_hi[:, place * CK + 2 * b:place * CK + 2 * b + 2, :],
                                   ps_t[:, b, :].rearrange("p (k c) -> p k c", k=2), ACT.Copy).then_inc(chT_hi_done, 1)

            def head_squares(h):
                act.wait_ge(pv_psum, h + 1)
                for t in range(TILES):
                    act.activation(gated[:, t, :], ps_t[:, t, :], ACT.Square,
                                   scale=RET_V ** -0.5, accum_out=mean_sq[:, t:t + 1])\
                        .then_inc(squares, 1)

            def take_v(v, h):
                for t in range(TILES):
                    act.wait_ge(tile_done, 2 * v.number + t + 1)
                    act.activation(v_sb[:, t, :], ps_proj[:, t, :], ACT.Copy).then_inc(v_ready, 1)

            def take_q(h):
                act.wait_ge(qkT_psum, h + 1)
                act.activation(qkT[:, 0, :, :], ps_t[:, 0, :].rearrange("p (e n) -> p e n", e=2), ACT.Copy)\
                    .then_inc(qT_ready, 1)

            def silu(g, t):
                act.wait_ge(tile_done, 2 * g.number + t + 1)
                act.activation(silu_g[:, t, :], ps_proj[:, t, :], ACT.Silu).then_inc(g_ready, 1)

            def ret_head(h, last=False):
                qk, v, g, o = ret_units(h)
                head_squares(h - 1)
                split_hi(v)
                take_chT(h - 1)
                split_hi(g)
                take_v(v, h)
                take_q(h)
                split_hi(o)
                silu(g, 0)
                silu(g, 1)
                if last:
                    head_squares(h)
                split_hi(Unit(RET_BASE + 3, 4, h))

            for t in range(TILES):
                take_xT(0, t)
            qk, v, g, _none = ret_units(0, first=True)
            for f in range(4):
                cols = slice(f * (UNIT // 4), (f + 1) * (UNIT // 4))
                act.wait_ge(first_landed[f], 16)
                act.activation(w_hi[:, v.slot, cols], raw[:, v.slot, cols], ACT.Copy)\
                    .then_inc(hi_done if f % 2 else first_hi, 1)
            split_hi(qk, wait=False)
            take_v(v, 0)
            split_hi(g)
            split_hi(ret_units(1)[0])
            take_q(0)
            silu(g, 0)
            silu(g, 1)
            with act.Fori(1, RET_HEADS - 1) as h:
                ret_head(h)
            ret_head(RET_HEADS - 1, last=True)
            take_chT(RET_HEADS - 1, place=1)

            def mlp(m):
                up, _none = mlp_units(m, 0, first=True)
                split_hi(up)
                for t in range(TILES):
                    take_xT(2 * m + 1, t)

                def relu(up, t):
                    act.wait_ge(tile_done, 2 * up.number + t + 1)
                    act.activation(hid[:, t, :], ps_proj[:, t, :], ACT.Relu).then_inc(relu_ready, 1)

                split_hi(mlp_units(m, 1)[0])
                for t in range(TILES):
                    relu(up, t)
                chunk0 = RET_HEADS + m * FF_CHUNKS

                def chunk(i, last=False):
                    up, down = mlp_units(m, i)
                    split_hi(down)
                    take_chT(chunk0 + i - 1)
                    relu(up, 0)
                    relu(up, 1)
                    split_hi(Unit(MLP_BASE[m] + 1, 2, i))

                with act.Fori(1, FF_CHUNKS - 1) as i:
                    chunk(i)
                chunk(FF_CHUNKS - 1)
                take_chT(chunk0 + FF_CHUNKS - 1, place=1)

            mlp(0)

            split_hi(dil_units(0, 0)[0])
            for t in range(TILES):
                take_xT(2, t)

            def copy_proj(unit, t, dst, done):
                act.wait_ge(tile_done, 2 * unit.number + t + 1)
                act.activation(dst[:, t], ps_proj[:, t, 0:DIL_COLS].rearrange("p (g c) -> p g c", g=NG), ACT.Copy)\
                    .then_inc(done, 1)

            def take_qT(p):
                act.wait_ge(dqkT_psum, p + 1)
                act.activation(qT.rearrange("p g n -> p (g n)"),
                               ps_acc[:, 0:2, :].rearrange("p b n -> p (b n)")[:, 0:NG * SEQ], ACT.Copy)\
                    .then_inc(dqT_ready, 1)

            def softmax_exp(p):
                for t, pt in ((0, p0), (1, p1)):
                    act.wait_ge(max_ready, TILES * p + t + 1)
                    act.activation(pt, pt, ACT.Exp, bias=neg_max[t], scale=DIL_SCALE, accum_out=row_sum[t])\
                        .then_inc(exp_ready, 1)

            def take_pT(p):
                act.wait_ge(pT_psum, p + 1)
                act.activation(pT[:, 0:2, :], ps_acc[:, 1:3, 0:3 * P], ACT.Copy).then_inc(pT_a_ready, 1)

            def take_oT(p):
                act.wait_ge(o_psum, p + 1)
                act.activation(oT_hi[:].rearrange("p h n -> p (h n)")[:, bass.ds(p * SEQ, SEQ)],
                               ps_acc[:, 0, 0:SEQ], ACT.Copy).then_inc(oT_hi_done, 1)

            def dil_head(pair, odd, first=False, last=False):
                h = 2 * pair + odd
                q, k, v = dil_units(pair, odd)
                if not first:
                    take_qT(h - 1)
                split_hi(k)
                copy_proj(q, 0, q_nat, q_taken)
                if not first:
                    softmax_exp(h - 1)
                copy_proj(q, 1, q_nat, q_taken)
                split_hi(v)
                if not first:
                    take_pT(h - 1)
                copy_proj(k, 0, k_nat, k_taken)
                copy_proj(k, 1, k_nat, k_taken)
                if not first:
                    take_oT(h - 1)
                if last:
                    split_hi(dil_out_units[0])
                else:
                    split_hi(next_dil_unit(pair, odd))
                copy_proj(v, 0, v_nat, v_taken)
                copy_proj(v, 1, v_nat, v_taken)

            dil_head(0, 0, first=True)
            with act.Fori(0, DIL_PAIRS - 1) as pair:
                dil_head(pair, 1)
                dil_head(pair + 1, 0)
            dil_head(DIL_PAIRS - 1, 1, last=True)
            take_qT(HEADS - 1)
            split_hi(dil_out_units[1])
            softmax_exp(HEADS - 1)
            take_pT(HEADS - 1)
            take_oT(HEADS - 1)

            mlp(1)

        @block.vector
        def _(dve):
            def split_lo(unit, halves=(0, 1)):
                half = unit.size // 2
                for f in halves:
                    cols = slice(f * half, (f + 1) * half)
                    dve.wait_ge(hi_done, 2 * unit.number + f + 1)
                    dve.tensor_tensor(w_lo[:, unit.slot, cols], raw[:, unit.slot, cols],
                                      w_hi[:, unit.slot, cols].bitcast(F32), ALU.subtract).then_inc(lo_done, 1)

            def take_xT(n, t):
                for b in range(2):
                    dve.wait_ge(xT_hi_done, 2 * TILES * n + 2 * t + b + 1)
                    s = slice(t * P, (t + 1) * P)
                    dve.tensor_tensor(xT_lo[:, 4 * b:4 * b + 4, s], ps_t[:, b, :].rearrange("p (k c) -> p k c", k=4),
                                      xT_hi[:, 4 * b:4 * b + 4, s].bitcast(F32), ALU.subtract).then_inc(xT_lo_done, 1)

            def take_chT(n, place=0):
                for b in range(2):
                    ks = slice(place * CK + 2 * b, place * CK + 2 * b + 2)
                    dve.wait_ge(chT_hi_done, 2 * n + b + 1)
                    dve.tensor_tensor(oT_lo[:, ks, :], ps_t[:, b, :].rearrange("p (k c) -> p k c", k=2),
                                      oT_hi[:, ks, :].bitcast(F32), ALU.subtract)\
                        .then_inc(chT_lo_done, 1)

            steps = [0]

            def ln_chain(ins):
                steps[0] += 1
                ins.then_inc(ln_step, 1)
                dve.wait_ge(ln_step, steps[0])

            def layer_norm(n, t, last_unit, src):
                row = x_res[:, t, :]
                for c in range(2):
                    if c == 0 and n != 2:
                        dve.wait_ge(acc_half, TILES * (n - (n > 2)) + t + 1)
                    elif c == 0:
                        dve.wait_ge(tile_done, 2 * dil_out_units[0].number + t + 1)
                    else:
                        dve.wait_ge(tile_done, 2 * last_unit.number + t + 1)
                    half = x_res[:, t, c * CH:(c + 1) * CH]
                    ins = dve.scalar_tensor_tensor(out=half, in0=half, scalar=ALPHA, in1=src(t, c),
                                                   op0=ALU.mult, op1=ALU.add)
                    ins.then_inc(acc_taken, 1)
                    dve.wait_ge(acc_taken, 2 * (TILES * n + t) + c + 1)
                    ln_chain(dve.bn_stats(stats[:, t, c, :], half))
                dve.bn_aggr(moments[:, t, :], stats[:, t, :, :]).then_inc(ln_moments, 1)
                dve.wait_ge(ln_moments, TILES * n + t + 1)
                dve.wait_ge(ln_landed[n % 2], 32 * (n // 2 + 1))
                ln_chain(dve.scalar_tensor_tensor(out=row, in0=row, scalar=moments[:, t, 0:1],
                                                  in1=ln_gb[:, n % 2, 0, :], op0=ALU.subtract, op1=ALU.mult))
                dve.wait_ge(ln_rstd, TILES * n + t + 1)
                for c in range(2):
                    cols = slice(c * CH, (c + 1) * CH)
                    dve.scalar_tensor_tensor(out=x_res[:, t, cols], in0=x_res[:, t, cols], scalar=rstd[t],
                                             in1=ln_gb[:, n % 2, 1, cols], op0=ALU.mult, op1=ALU.add)\
                        .then_inc(x_ready, 1)

            def rotate(qk, t, h):
                dve.wait_ge(tile_done, 2 * qk.number + t + 1)
                c = TILES * h + t
                pairs = ps_proj[:, t, :].rearrange("p (c e) -> p e c", e=2)
                cos = ret_rot[:, t, 0:1, :].to_broadcast([P, 2, 2 * RET_HALF])
                sin = ret_rot[:, t, 1:2, :].to_broadcast([P, 2, 2 * RET_HALF])
                mc, ms = even_odd(rot_c), even_odd(rot_s)
                dve.tensor_tensor(mc, pairs, cos, ALU.mult).then_inc(rot_step, 1)
                dve.tensor_tensor(ms, pairs, sin, ALU.mult).then_inc(qk_taken, 1)
                dve.wait_ge(rot_step, 2 * c + 1)
                dve.wait_ge(qk_taken, c + 1)
                dve.tensor_tensor(rot[:, t, 0, :], mc[:, 0], ms[:, 1], ALU.subtract).then_inc(rot_step, 1)
                dve.tensor_tensor(rot[:, t, 1, :], mc[:, 1], ms[:, 0], ALU.add).then_inc(rot_ready, 1)
                dve.wait_ge(rot_step, 2 * c + 2)
                dve.wait_ge(rot_ready, c + 1)

            def gate(h):
                dve.wait_ge(gn_ready, h + 1)
                for t in range(TILES):
                    dve.wait_ge(g_ready, TILES * h + t + 1)
                    dve.scalar_tensor_tensor(out=gated[:, t, :], in0=ps_t[:, t, :], scalar=gn_rstd[:, t:t + 1],
                                             in1=silu_g[:, t, :], op0=ALU.mult, op1=ALU.mult)\
                        .then_inc(gated_ready, 1)

            def take_k(h):
                dve.wait_ge(qkT_psum, h + 1)
                dve.tensor_copy(qkT[:, 1, :, :], ps_t[:, 1, :].rearrange("p (e n) -> p e n", e=2))\
                    .then_inc(kT_ready, 1)

            def take_scores(h):
                dve.wait_ge(s_psum, h + 1)
                dve.tensor_tensor(sT, ps_t[:, 0, 0:3 * P], decay[:, bass.ds(h * 3 * P, 3 * P)], ALU.mult)\
                    .then_inc(sT_ready, 1)

            def ret_head(h, last=False):
                qk, v, g, o = ret_units(h)
                gate(h - 1)
                split_lo(v)
                rotate(qk, 0, h)
                rotate(qk, 1, h)
                take_chT(h - 1)
                split_lo(g)
                take_k(h)
                split_lo(o, halves=(0,))
                take_scores(h)
                split_lo(o, halves=(1,))
                if last:
                    gate(h)
                split_lo(Unit(RET_BASE + 3, 4, h))

            for t in range(TILES):
                take_xT(0, t)
            qk, v, g, _none = ret_units(0, first=True)
            for f in range(4):
                cols = slice(f * (UNIT // 4), (f + 1) * (UNIT // 4))
                dve.wait_ge(hi_done if f % 2 else first_hi, f // 2 + 1)
                dve.tensor_tensor(w_lo[:, v.slot, cols], raw[:, v.slot, cols], w_hi[:, v.slot, cols].bitcast(F32),
                                  ALU.subtract).then_inc(lo_done if f % 2 else first_lo, 1)
            split_lo(qk)
            dve.wait_ge(tables_landed, 16 * 2)
            split_lo(g)
            rotate(qk, 0, 0)
            rotate(qk, 1, 0)
            split_lo(ret_units(1)[0], halves=(0,))
            take_k(0)
            split_lo(ret_units(1)[0], halves=(1,))
            take_scores(0)
            with dve.Fori(1, RET_HEADS - 1) as h:
                ret_head(h)
            ret_head(RET_HEADS - 1, last=True)
            take_chT(RET_HEADS - 1, place=1)

            def norm_and_transpose(n, last_unit, src):
                for t in range(TILES):
                    layer_norm(n, t, last_unit, src)
                    take_xT(n + 1, t)

            def mlp(m, last_unit, src):
                up, _none = mlp_units(m, 0, first=True)
                split_lo(up)
                norm_and_transpose(2 * m, last_unit, src)

                def square(t, n):
                    dve.wait_ge(relu_ready, TILES * n + t + 1)
                    dve.tensor_tensor(hid_sq[:, t, :], hid[:, t, :], hid[:, t, :], ALU.mult).then_inc(hid_ready, 1)

                n0 = m * FF_CHUNKS
                split_lo(mlp_units(m, 1)[0])
                square(0, n0)
                square(1, n0)

                def chunk(i):
                    up, down = mlp_units(m, i)
                    split_lo(down)
                    take_chT(RET_HEADS + n0 + i - 1)
                    square(0, n0 + i)
                    square(1, n0 + i)
                    split_lo(Unit(MLP_BASE[m] + 1, 2, i))

                with dve.Fori(1, FF_CHUNKS - 1) as i:
                    chunk(i)
                chunk(FF_CHUNKS - 1)
                take_chT(RET_HEADS + n0 + FF_CHUNKS - 1, place=1)

            mlp(0, ret_last_out, acc)

            split_lo(dil_units(0, 0)[0])
            norm_and_transpose(1, mlp_last_down(0), acc)
            dve.wait_ge(tables_landed, 16 * 4)

            def rope(nat, h, is_k, roped):
                n = 2 * h + is_k
                x12 = nat[:, :, :, 0:ROT]
                cos = dil_rot[:, :, 0:1, :].to_broadcast([P, TILES, NG, ROT])
                sin = dil_rot[:, :, 1:2, :].to_broadcast([P, TILES, NG, ROT])
                hr = ROT // 2
                dve.tensor_tensor(dil_c, x12, cos, ALU.mult).then_inc(rope_step, 1)
                dve.tensor_tensor(dil_s, x12, sin, ALU.mult).then_inc(rope_step, 1)
                dve.wait_ge(rope_step, 3 * n + 2)
                dve.tensor_tensor(nat[:, :, :, 0:hr], dil_c[:, :, :, 0:hr], dil_s[:, :, :, hr:ROT], ALU.subtract)\
                    .then_inc(rope_step, 1)
                dve.tensor_tensor(nat[:, :, :, hr:ROT], dil_c[:, :, :, hr:ROT], dil_s[:, :, :, 0:hr], ALU.add)\
                    .then_inc(roped, 1)
                dve.wait_ge(rope_step, 3 * n + 3)
                dve.wait_ge(roped, h + 1)

            def take_kT(p):
                dve.wait_ge(dqkT_psum, p + 1)
                dve.tensor_copy(kT.rearrange("p g n -> p (g n)"),
                                ps_acc[:, 2:4, :].rearrange("p b n -> p (b n)")[:, 0:NG * SEQ])\
                    .then_inc(dkT_ready, 1)

            def softmax_max(p):
                parts = ((0, p0, ps_acc[:, 0, 0:S0], mask[:, 0:S0]),
                         (1, p1, ps_t[:].rearrange("p b n -> p (b n)")[:, 0:S1], mask[:, S0:]))
                for t, pt, scores, m in parts:
                    dve.wait_ge(scores_psum, TILES * p + t + 1)
                    dve.memset(wait_cell[t], 0.0)
                    dve.tensor_tensor_reduce(pt, scores, m, 1.0, -3.0e38, ALU.add, ALU.max, row_max[t])\
                        .then_inc(masked, 1)
                    dve.wait_ge(masked, TILES * p + t + 1)
                    dve.tensor_scalar(neg_max[t], row_max[t], -DIL_SCALE, None, ALU.mult).then_inc(max_ready, 1)

            def softmax_norm(p):
                for t, pt in ((0, p0), (1, p1)):
                    dve.wait_ge(exp_ready, TILES * p + t + 1)
                    dve.reciprocal(row_inv[t], row_sum[t]).then_inc(inv_ready, 1)
                    dve.wait_ge(inv_ready, TILES * p + t + 1)
                    dve.tensor_scalar(pt, pt, row_inv[t], None, ALU.mult).then_inc(probs_ready, 1)

            def take_pT(p):
                dve.wait_ge(pT_psum, p + 1)
                dve.tensor_copy(pT[:, 2, :], ps_acc[:, 3, 0:3 * P]).then_inc(pT_b_ready, 1)

            def take_oT(p):
                dve.wait_ge(oT_hi_done, p + 1)
                cols = bass.ds(p * SEQ, SEQ)
                dve.tensor_tensor(oT_lo[:].rearrange("p h n -> p (h n)")[:, cols], ps_acc[:, 0, 0:SEQ],
                                  oT_hi[:].rearrange("p h n -> p (h n)")[:, cols].bitcast(F32), ALU.subtract)\
                    .then_inc(oT_lo_done, 1)

            def dil_head(pair, odd, first=False, last=False):
                h = 2 * pair + odd
                q, k, v = dil_units(pair, odd)
                if not first:
                    take_kT(h - 1)
                split_lo(k)
                if not first:
                    softmax_max(h - 1)
                    softmax_norm(h - 1)
                dve.wait_ge(q_taken, TILES * (h + 1))
                rope(q_nat, h, 0, q_roped)
                split_lo(v)
                if not first:
                    take_pT(h - 1)
                dve.wait_ge(k_taken, TILES * (h + 1))
                rope(k_nat, h, 1, k_roped)
                if not first:
                    take_oT(h - 1)
                if last:
                    split_lo(dil_out_units[0])
                else:
                    split_lo(next_dil_unit(pair, odd))

            dil_head(0, 0, first=True)
            with dve.Fori(0, DIL_PAIRS - 1) as pair:
                dil_head(pair, 1)
                dil_head(pair + 1, 0)
            dil_head(DIL_PAIRS - 1, 1, last=True)
            take_kT(HEADS - 1)
            split_lo(dil_out_units[1])
            softmax_max(HEADS - 1)
            softmax_norm(HEADS - 1)
            take_pT(HEADS - 1)
            take_oT(HEADS - 1)

            mlp(1, dil_out_units[1], dil_out)
            for t in range(TILES):
                layer_norm(2 * DEPTH - 1, t, mlp_last_down(1), acc)

        @block.tensor
        def _(pe):
            def product(dst, hi, lo, whi, wlo, start, stop):
                pe.matmul(dst, hi, whi, start=start, stop=False)
                pe.matmul(dst, hi, wlo, start=False, stop=False)
                return pe.matmul(dst, lo, whi, start=False, stop=stop)

            def open_accumulators(banks):
                for bank in banks:
                    pe.matmul(bank, zeros[:, 0:P], zeros[:], start=True, stop=False)

            def wide(unit, t, ks, xh, xl, dst, cols, wait=True, done=tile_done, new_x=None):
                half = KT // 2

                def tile(w, k):
                    if unit.blocks == 1:
                        return w[:, unit.slot, k * cols:(k + 1) * cols]
                    blocks = w[:, unit.slot, 0:unit.size].rearrange("p (b k c) -> p k b c", b=unit.blocks, k=KT)
                    return blocks[:, k]

                for k in ks:
                    if wait and unit.blocks == 1 and k % half == 0:
                        pe.wait_ge(lo_done, 2 * unit.number + k // half + 1)
                    elif wait and k == 0:
                        pe.wait_ge(lo_done, 2 * unit.number + 2)
                    if new_x is not None and k % half == 0:
                        pe.wait_ge(xT_lo_done, 2 * (TILES * new_x + t) + k // half + 1)
                    x_ = slice(t * P, (t + 1) * P)
                    last = product(dst, xh[:, k, x_], xl[:, k, x_], tile(w_hi, k), tile(w_lo, k),
                                   start=(k == 0), stop=(k == KT - 1))
                if done is not None:
                    last.then_inc(done, 1)

            def project(unit, t, cols, new_x=None, ks=range(KT)):
                wide(unit, t, ks, xT_hi, xT_lo, ps_proj[:, t, 0:cols], cols, wait=(t == 0),
                     done=tile_done if ks[-1] == KT - 1 else None, new_x=new_x)

            def accumulate(unit, t, place=0, last_of_stage=False):
                order = [(k, n) for k in range(CK) for n in range(2)]
                if last_of_stage:
                    order.sort(key=lambda kn: kn[1])
                for k, n in order:
                    if t == 0 and n == 0 and k % 2 == 0:
                        pe.wait_ge(lo_done, 2 * unit.number + k // 2 + 1)
                    w = slice(k * D_MODEL + n * CH, k * D_MODEL + (n + 1) * CH)
                    x_ = slice(t * P, (t + 1) * P)
                    last = product(acc(t, n), oT_hi[:, place * CK + k, x_], oT_lo[:, place * CK + k, x_],
                                   w_hi[:, unit.slot, w], w_lo[:, unit.slot, w],
                                   start=False, stop=(last_of_stage and k == CK - 1))
                    if last_of_stage and (k, n) == (CK - 1, 0):
                        last.then_inc(acc_half, 1)
                last.then_inc(tile_done, 1)

            def transpose_x(n, t):
                for k in range(KT):
                    b = k // 4
                    if k % 4 == 0:
                        if n:
                            pe.wait_ge(x_ready, 2 * (TILES * (n - 1) + t) + b + 1)
                        if t:
                            pe.wait_ge(xT_lo_done, 2 * TILES * n + b + 1)
                    last = pe.transpose(ps_t[:, b, (k % 4) * P:(k % 4 + 1) * P],
                                        x_res[:, t, k * P:(k + 1) * P], ident[:])
                    if k % 4 == 3:
                        last.then_inc(xT_psum, 1)

            def transpose_chunk(src):
                for k in range(CK):
                    for t in range(TILES):
                        c = (k % 2) * SEQ + t * P
                        last = pe.transpose(ps_t[:, k // 2, c:c + P], src[:, t, k * P:(k + 1) * P], ident[:])
                    if k % 2 == 1:
                        last.then_inc(chT_psum, 1)

            pe.wait_ge(const_done, 4)
            open_accumulators([acc(t, n) for t in range(TILES) for n in range(2)])
            pe.wait_ge(ident_landed, 16)
            for t in range(TILES):
                pe.wait_ge(x_landed[t], 16)
                transpose_x(0, t)

            def transpose_gated(h):
                pe.wait_ge(gated_ready, TILES * (h + 1))
                transpose_chunk(gated)

            def project_taken(unit, taken, h):
                for t in range(TILES):
                    pe.wait_ge(taken, TILES * h + t + 1)
                    project(unit, t, CH)

            def transpose_rotated():
                for s in range(2):
                    for e in range(2):
                        for t in range(TILES):
                            last = pe.transpose(ps_t[:, s, e * SEQ + t * P:e * SEQ + (t + 1) * P],
                                                rot[:, t, e, s * RET_HALF:(s + 1) * RET_HALF], ident[:])
                last.then_inc(qkT_psum, 1)

            def ret_scores(h):
                pe.wait_ge(qT_ready, h + 1)
                pe.wait_ge(kT_ready, h + 1)
                for dst, keys, queries in ((slice(0, SEQ), slice(0, P), slice(0, SEQ)),
                                           (slice(SEQ, SEQ + P), slice(P, SEQ), slice(P, SEQ))):
                    for e in range(2):
                        last = pe.matmul(ps_t[:, 0, dst], qkT[:, 1, e, keys], qkT[:, 0, e, queries],
                                         start=(e == 0), stop=(e == 1))
                last.then_inc(s_psum, 1)

            def gate_and_scores(g, h):
                pe.wait_ge(v_ready, TILES * h + 1)
                project(g, 0, CH)
                ret_scores(h)
                pe.wait_ge(v_ready, TILES * h + 2)
                project(g, 1, CH)

            def ret_values(h):
                pe.wait_ge(sT_ready, h + 1)
                pe.matmul(ps_t[:, 0, :], sT[:, 0:P], v_sb[:, 0, :], start=True, stop=True)
                pe.matmul(ps_t[:, 1, :], sT[:, P:SEQ], v_sb[:, 0, :], start=True, stop=False)
                pe.matmul(ps_t[:, 1, :], sT[:, SEQ:SEQ + P], v_sb[:, 1, :], start=False, stop=True)\
                    .then_inc(pv_psum, 1)

            def ret_head(h, last=False):
                qk, v, g, o = ret_units(h)
                project_taken(qk, g_ready, h - 1)
                transpose_gated(h - 1)
                project_taken(v, qk_taken, h)
                pe.wait_ge(rot_ready, TILES * (h + 1))
                pe.wait_ge(chT_lo_done, 2 * h)
                transpose_rotated()
                gate_and_scores(g, h)
                if last:
                    ret_values(h)
                    accumulate(o, 0)
                    transpose_gated(h)
                    accumulate(o, 1)
                else:
                    accumulate(o, 0)
                    accumulate(o, 1)
                    ret_values(h)

            qk, v, g, _none = ret_units(0, first=True)
            for t in range(TILES):
                for f in range(4):
                    if t == 0:
                        pe.wait_ge(lo_done if f % 2 else first_lo, f // 2 + 1)
                    wide(v, t, range(2 * f, 2 * f + 2), xT_hi, xT_lo, ps_proj[:, t, :], CH, wait=False,
                         done=tile_done if f == 3 else None, new_x=0)
            project_taken(qk, v_ready, 0)
            pe.wait_ge(qk_taken, 1)
            project(g, 0, CH)
            pe.wait_ge(rot_ready, TILES)
            transpose_rotated()
            pe.wait_ge(qk_taken, 2)
            project(g, 1, CH)
            ret_scores(0)
            ret_values(0)
            with pe.Fori(1, RET_HEADS - 1) as h:
                ret_head(h)
            ret_head(RET_HEADS - 1, last=True)
            pe.wait_ge(chT_lo_done, 2 * RET_HEADS)
            accumulate(ret_last_out, 0, place=1, last_of_stage=True)
            accumulate(ret_last_out, 1, place=1, last_of_stage=True)

            SEAM = 6

            def first_unit(unit, n, cols, open_acc):
                transpose_x(n, 0)
                if open_acc:
                    open_accumulators([acc(0, c) for c in range(2)])
                project(unit, 0, cols, new_x=n, ks=range(SEAM))
                transpose_x(n, 1)
                project(unit, 0, cols, new_x=n, ks=range(SEAM, KT))
                if open_acc:
                    open_accumulators([acc(1, c) for c in range(2)])
                project(unit, 1, cols, new_x=n)

            def mlp(m):
                up, _none = mlp_units(m, 0, first=True)
                first_unit(up, 2 * m + 1, CH, open_acc=True)
                n0 = m * FF_CHUNKS

                def transpose_hidden(i):
                    pe.wait_ge(hid_ready, TILES * (n0 + i + 1))
                    transpose_chunk(hid_sq)

                def chunk(i, last=False):
                    up, down = mlp_units(m, i)
                    pe.wait_ge(relu_ready, TILES * (n0 + i - 1) + 1)
                    project(up, 0, CH)
                    transpose_hidden(i - 1)
                    project(up, 1, CH)
                    pe.wait_ge(chT_lo_done, 2 * (RET_HEADS + n0 + i))
                    accumulate(down, 0)
                    if last:
                        transpose_hidden(i)
                    accumulate(down, 1)

                with pe.Fori(1, FF_CHUNKS - 1) as i:
                    chunk(i)
                chunk(FF_CHUNKS - 1, last=True)
                pe.wait_ge(chT_lo_done, 2 * (RET_HEADS + n0 + FF_CHUNKS))
                for t in range(TILES):
                    accumulate(mlp_last_down(m), t, place=1, last_of_stage=True)

            mlp(0)

            def transpose_qk(p):
                pe.wait_ge(q_roped, p + 1)
                pe.wait_ge(k_roped, p + 1)
                for first_bank, nat in ((0, q_nat), (2, k_nat)):
                    for g in range(NG):
                        for t in range(TILES):
                            b = TILES * g + t
                            c = (b % 4) * P
                            last = pe.transpose(ps_acc[:, first_bank + b // 4, c:c + P], nat[:, t, g, :], ident[:])
                last.then_inc(dqkT_psum, 1)

            def scores(p):
                pe.wait_ge(dqT_ready, p + 1)
                pe.wait_ge(dkT_ready, p + 1)
                for g in range(NG):
                    last = pe.matmul(ps_acc[:, 0, g * P:(g + 1) * P], qT[:, g, 0:P], kT[:, g, 0:P],
                                     start=True, stop=True)
                last.then_inc(scores_psum, 1)
                for g in range(NG):
                    c = (g % 2) * SEQ
                    last = pe.matmul(ps_t[:, g // 2, c:c + SEQ], qT[:, g, P:SEQ], kT[:, g, :],
                                     start=True, stop=True)
                last.then_inc(scores_psum, 1)

            def transpose_probs(p):
                pe.wait_ge(probs_ready, TILES * (p + 1))
                for g in range(NG):
                    parts = (p0[:, g * P:(g + 1) * P], p1[:, g * SEQ:g * SEQ + P], p1[:, g * SEQ + P:(g + 1) * SEQ])
                    for b, part in enumerate(parts):
                        last = pe.transpose(ps_acc[:, 1 + g, b * P:(b + 1) * P], part, ident[:])
                last.then_inc(pT_psum, 1)

            def values(p):
                pe.wait_ge(v_taken, TILES * (p + 1))
                pe.wait_ge(pT_a_ready, p + 1)
                pe.wait_ge(pT_b_ready, p + 1)
                for g in range(NG):
                    pe.matmul(ps_acc[:, 0, 0:SEQ], v_nat[:, 0, g, :], pT[:, g, 0:SEQ],
                              start=(g == 0), stop=False, skip_group_check=True)
                    last = pe.matmul(ps_acc[:, 0, P:SEQ], v_nat[:, 1, g, :], pT[:, g, SEQ:SEQ + P],
                                     start=False, stop=(g == NG - 1), skip_group_check=True)
                last.then_inc(o_psum, 1)

            def dil_head(pair, odd, first=False):
                h = 2 * pair + odd
                q, k, v = dil_units(pair, odd)
                if first:
                    first_unit(q, 2, DIL_COLS, open_acc=False)
                else:
                    if not (isinstance(h, int) and h == 1):
                        pe.wait_ge(oT_lo_done, h - 1)
                    transpose_qk(h - 1)
                    pe.wait_ge(v_taken, TILES * (h - 1) + 1)
                    project(q, 0, DIL_COLS)
                    scores(h - 1)
                    pe.wait_ge(v_taken, TILES * h)
                    project(q, 1, DIL_COLS)
                pe.wait_ge(q_taken, TILES * h + 1)
                project(k, 0, DIL_COLS)
                if not first:
                    transpose_probs(h - 1)
                pe.wait_ge(q_taken, TILES * (h + 1))
                project(k, 1, DIL_COLS)
                if not first:
                    values(h - 1)
                for t in range(TILES):
                    pe.wait_ge(k_taken, TILES * h + t + 1)
                    project(v, t, DIL_COLS)

            dil_head(0, 0, first=True)
            with pe.Fori(0, DIL_PAIRS - 1) as pair:
                dil_head(pair, 1)
                dil_head(pair + 1, 0)
            dil_head(DIL_PAIRS - 1, 1)
            last_h = HEADS - 1
            pe.wait_ge(oT_lo_done, last_h)
            transpose_qk(last_h)
            pe.wait_ge(v_taken, TILES * HEADS)
            o0, o1 = dil_out_units
            wide(o0, 0, range(KT - 1), oT_hi, oT_lo, dil_out(0, 0), CH, done=None)
            scores(last_h)
            wide(o0, 1, range(KT - 3), oT_hi, oT_lo, dil_out(1, 0), CH, wait=False, done=None)
            transpose_probs(last_h)
            wide(o0, 1, range(KT - 3, KT - 1), oT_hi, oT_lo, dil_out(1, 0), CH, wait=False, done=None)
            values(last_h)
            pe.wait_ge(oT_lo_done, HEADS)
            wide(o0, 0, [KT - 1], oT_hi, oT_lo, dil_out(0, 0), CH, wait=False)
            wide(o0, 1, [KT - 1], oT_hi, oT_lo, dil_out(1, 0), CH, wait=False)
            wide(o1, 0, range(KT), oT_hi, oT_lo, dil_out(0, 1), CH)
            wide(o1, 1, range(KT), oT_hi, oT_lo, dil_out(1, 1), CH, wait=False)

            mlp(1)


_INS = ["x", "ret_w_in", "ret_w_out", "kv_w", "dil_w_q", "dil_w_out", "mlp_w_up", "mlp_w_down", "ln_g", "ln_b"]


def kernel(**inputs):
    import concourse.bacc as bacc
    from concourse.bass_utils import run_bass_kernel_spmd

    nc = bacc.Bacc("TRN2", target_bir_lowering=False, num_devices=1)
    arrays = {name: np.ascontiguousarray(inputs[name]) for name in _INS}
    arrays.update({name: np.ascontiguousarray(a) for name, a in stage_tables().items()})
    args = [nc.dram_tensor(f"in_{name}", a.shape, F32, kind="ExternalInput").ap() for name, a in arrays.items()]
    out = nc.dram_tensor("out", (1, SEQ, D_MODEL), F32, kind="ExternalOutput").ap()
    trunk(nc, *args, out)
    r = run_bass_kernel_spmd(nc, [{f"in_{name}": a for name, a in arrays.items()}], core_ids=[0])
    return r.results[0]["out"]
```

```python
import math
from contextlib import ExitStack

import numpy as np

import concourse.bass as bass
from concourse import mybir

F32 = mybir.dt.float32
F32R = mybir.dt.float32r
BF16 = mybir.dt.bfloat16
ALU = mybir.AluOpType
ACT = mybir.ActivationFunctionType

P = 128
D_MODEL = 1024
SEQ = 256
TILES = SEQ // P
KT = D_MODEL // P
DEPTH = 2
ALPHA = (2.0 * DEPTH) ** 0.25
LN_EPS = 1e-5
GN_EPS = 1e-6

RET_HEADS = 4
RET_QK = D_MODEL // RET_HEADS
RET_V = 2 * RET_QK
RET_HALF = RET_QK // 2

GROUPS = ((128, 1), (512, 4), (2048, 16))
NG = len(GROUPS)
HEADS = 8
HD = D_MODEL // HEADS
ROT = HD // 4
DIL_SCALE = float(HD) ** -0.5

D_FF = 4 * D_MODEL
CH = 512
FF_CHUNKS = D_FF // CH
CK = CH // P

UNIT = KT * CH
DIL_COLS = NG * HD
DIL_UNIT = KT * DIL_COLS

RET_UNITS = 4 * RET_HEADS
MLP_UNITS = 2 * FF_CHUNKS
DIL_UNITS = 3 * HEADS + 2
RET_BASE = 0
MLP_BASE = (RET_BASE + RET_UNITS, RET_BASE + RET_UNITS + MLP_UNITS + DIL_UNITS)
DIL_BASE = RET_BASE + RET_UNITS + MLP_UNITS

FIRST_PIECES = ((0, 1), (1, 2), (2, 4), (4, 6), (6, 8))


def piece_count(i, inner, halves):
    ends = [p[1] % (KT // 2) == 0 for p in FIRST_PIECES]
    return (halves if ends[i] else inner), sum(e == ends[i] for e in ends[:i + 1])


S0 = NG * P
S1 = NG * SEQ


class Unit:

    def __init__(self, a, b=0, i=0, size=UNIT, blocks=1):
        assert b % 2 == 0
        self.slot = a % 2
        self.number = a + b * i
        self.size = size
        self.blocks = blocks
        if blocks == NG:
            self.turn = (a - DIL_BASE) // 2 + (b // 2) * i
        else:
            self.turn = a // 2 + (b // 2) * i - (3 * HEADS // 2 if a > DIL_BASE else 0) - 1


def stage_tables():
    f = np.float32
    pos = np.arange(SEQ, dtype=f)
    angle = (f(1.0) / (f(10000.0) ** np.linspace(0.0, 1.0, RET_HALF, dtype=f))).astype(f)
    ang = pos[:, None] * angle[None]
    ret = np.stack([np.cos(ang), np.sin(ang)], 1).astype(f)
    ret = np.concatenate([ret, ret], -1)
    ret = ret.reshape(TILES, P, 2, 2 * RET_HALF).transpose(1, 0, 2, 3)

    inv = (f(500000.0) ** (-np.arange(0, ROT, 2, dtype=f) / f(ROT))).astype(f)
    ang = pos[:, None] * inv[None]
    dil = np.stack([np.cos(ang), np.sin(ang)], 1).astype(f)
    dil = np.concatenate([dil, dil], -1)
    dil = dil.reshape(TILES, P, 2, ROT).transpose(1, 0, 2, 3)

    log_g = np.log(f(1.0) - f(2.0) ** (f(-5.0) - np.arange(RET_HEADS, dtype=f))).astype(f)
    j = np.arange(P, dtype=f)[:, None]
    i = np.arange(P, dtype=f)[None]
    decay = np.zeros((P, RET_HEADS, 3 * P), f)
    for h in range(RET_HEADS):
        inside = np.where(i >= j, np.exp(np.maximum(i - j, f(0)) * log_g[h]), f(0))
        across = np.exp((i + 1) * log_g[h]) * np.exp((P - 1 - j) * log_g[h])
        decay[:, h] = np.concatenate([inside, across, inside], 1) * f(RET_QK) ** f(-0.5)

    q = np.arange(SEQ)[:, None]
    k = np.arange(SEQ)[None]
    mask = np.zeros((P, S0 + S1), f)
    for g, (window, dilation) in enumerate(GROUPS):
        seen = (q >= k) & ((q - k) % dilation == 0) & (q - k <= window)
        m = np.where(seen, f(0), f(-1e30))
        mask[:, g * P:(g + 1) * P] = m[:P, :P]
        mask[:, S0 + g * SEQ:S0 + (g + 1) * SEQ] = m[P:]
    return {"ret_rot": ret, "dil_rot": dil, "decay": decay, "mask": mask, "ident": np.eye(P, dtype=f)}


def trunk(nc, x, ret_w_in, ret_w_out, kv_w, dil_w_q, dil_w_out, mlp_w_up, mlp_w_down, ln_g, ln_b,
          ret_rot_d, dil_rot_d, decay_d, mask_d, ident_d, out):
    with ExitStack() as ctx:
        def sb(name, shape, dt=F32):
            return ctx.enter_context(nc.sbuf_tensor(name, shape, dt))

        def sem(name):
            return ctx.enter_context(nc.semaphore(name))

        raw = sb("raw", [P, 2, UNIT])
        w_hi = sb("w_hi", [P, 2, UNIT], F32R)
        w_lo = sb("w_lo", [P, 2, UNIT], F32R)
        x_res = sb("x_res", [P, TILES, D_MODEL])
        xT_hi = sb("xT_hi", [P, KT, SEQ], F32R)
        xT_lo = sb("xT_lo", [P, KT, SEQ], F32R)
        oT_hi = sb("oT_hi", [P, HEADS, SEQ], F32R)
        oT_lo = sb("oT_lo", [P, HEADS, SEQ], F32R)
        ln_gb = sb("ln_gb", [P, 2, D_MODEL])
        ret_rot = sb("ret_rot", [P, TILES, 2, 2 * RET_HALF])
        dil_rot = sb("dil_rot", [P, TILES, 2, ROT])
        decay = sb("decay", [P, RET_HEADS * 3 * P])
        mask = decay[:, 0:S0 + S1]
        ident = sb("ident", [P, P])
        zeros = sb("zeros", [P, CH], BF16)
        stats = sb("stats", [P, TILES, 2, 6])
        moments = sb("moments", [P, TILES, 2])
        small = sb("small", [P, 32])
        neg_half = small[:, 0:1]
        var_eps = [small[:, 1 + t:2 + t] for t in range(TILES)]
        rstd = [small[:, 3 + t:4 + t] for t in range(TILES)]
        mean_sq = small[:, 5:5 + TILES]
        gn_eps_c = small[:, 21:21 + TILES]
        wait_cell = [small[:, 23 + t:24 + t] for t in range(TILES)]
        ms_eps = small[:, 7:7 + TILES]
        gn_rstd = small[:, 9:9 + TILES]
        neg_half2 = small[:, 11:11 + TILES]
        row_max = [small[:, 13 + t:14 + t] for t in range(TILES)]
        neg_max = [small[:, 15 + t:16 + t] for t in range(TILES)]
        row_sum = [small[:, 17 + t:18 + t] for t in range(TILES)]
        row_inv = [small[:, 19 + t:20 + t] for t in range(TILES)]

        arena = sb("arena", [P, 4992])
        arena_r = sb("arena_r", [P, 4608], F32R)
        at = {"f": 0, "r": 0}

        def view(cols, a="f"):
            at[a] += cols
            return (arena if a == "f" else arena_r)[:, at[a] - cols:at[a]]

        def even_odd(ap):
            return ap.rearrange("p (e c) -> p e c", e=2)

        rot_c = view(2 * RET_QK)
        rot_s = view(2 * RET_QK)
        rot = view(TILES * 2 * RET_QK).rearrange("p (t e c) -> p t e c", t=TILES, e=2)
        silu_g = view(TILES * RET_V).rearrange("p (t c) -> p t c", t=TILES)
        sT = view(3 * P)
        gated = view(TILES * RET_V).rearrange("p (t c) -> p t c", t=TILES)
        q1T, k1T = [view(2 * P).rearrange("p (e n) -> p e n", e=2) for _which in range(2)]
        qT_hi, qT_lo = [view(2 * SEQ, "r").rearrange("p (e n) -> p e n", e=2) for _part in range(2)]
        k0T_hi, k0T_lo = [view(2 * P, "r").rearrange("p (e n) -> p e n", e=2) for _part in range(2)]
        v_hi, v_lo = [view(TILES * RET_V, "r").rearrange("p (t c) -> p t c", t=TILES) for _part in range(2)]
        sT_hi, sT_lo = [view(3 * P, "r") for _part in range(2)]
        at = {"f": 0, "r": 0}
        hid = view(TILES * CH).rearrange("p (t c) -> p t c", t=TILES)
        hid_sq = view(TILES * CH).rearrange("p (t c) -> p t c", t=TILES)
        at = {"f": 0, "r": 0}
        q_nat = view(TILES * DIL_COLS).rearrange("p (t g c) -> p t g c", t=TILES, g=NG)
        k_nat = view(TILES * DIL_COLS).rearrange("p (t g c) -> p t g c", t=TILES, g=NG)
        probs = view(S0 + S1)
        p0 = probs[:, 0:S0]
        p1 = probs[:, S0:]
        dil_c = view(TILES * NG * ROT).rearrange("p (t g c) -> p t g c", t=TILES, g=NG)
        dil_s = view(TILES * NG * ROT).rearrange("p (t g c) -> p t g c", t=TILES, g=NG)
        dq0T, dk0T, dv1, p11T = [view(DIL_COLS).rearrange("p (g n) -> p g n", g=NG) for _which in range(4)]
        dq1T_hi, dq1T_lo, dv0_hi, dv0_lo = [view(DIL_COLS, "r").rearrange("p (g n) -> p g n", g=NG)
                                            for _part in range(4)]
        dkT_hi, dkT_lo, pT_hi, pT_lo = [view(NG * SEQ, "r").rearrange("p (g n) -> p g n", g=NG)
                                        for _part in range(4)]

        ps_proj = ctx.enter_context(nc.psum_tensor("ps_proj", [P, TILES, CH], F32))
        ps_t = ctx.enter_context(nc.psum_tensor("ps_t", [P, 2, CH], F32))
        ps_acc = ctx.enter_context(nc.psum_tensor("ps_acc", [P, 4, CH], F32))

        def acc(t, n):
            return ps_acc[:, 2 * t + n, :]

        def pT_bank(b):
            return ps_acc[:, 1 + b, 0:(2 - b) * SEQ].rearrange("p (g n) -> p g n", g=2 - b)

        def dil_out(t, n):
            return ps_proj[:, t, :] if n == 0 else ps_acc[:, 1 + t, :]

        raw_landed = [[sem(f"raw_landed_{s}{f}") for f in range(2)] for s in range(2)]
        first_landed = [sem(f"first_landed_{i}") for i in range(len(FIRST_PIECES))]
        second_landed = [sem(f"second_landed_{f}") for f in range(2)]
        dil_landed = [sem(f"dil_landed_{s}") for s in range(2)]
        x_landed = [sem(f"x_landed_{t}") for t in range(TILES)]
        ident_landed = sem("ident_landed")
        tables_landed = sem("tables_landed")
        ln_landed = sem("ln_landed")
        out_landed = sem("out_landed")
        first_hi = sem("first_hi")
        first_lo = sem("first_lo")
        hi_done = sem("hi_done")
        lo_done = sem("lo_done")
        quarter_lo = sem("quarter_lo")
        tile_done = sem("tile_done")
        const_done = sem("const_done")
        xT_psum = sem("xT_psum")
        xT_hi_done = sem("xT_hi_done")
        xT_lo_done = sem("xT_lo_done")
        acc_half = sem("acc_half")
        ln_summed = sem("ln_summed")
        ln_counted = sem("ln_counted")
        ln_moments = sem("ln_moments")
        ln_gained = sem("ln_gained")
        ln_eps = sem("ln_eps")
        ln_rstd = sem("ln_rstd")
        x_ready = sem("x_ready")
        rot_step = sem("rot_step")
        qk_taken = sem("qk_taken")
        rot_ready = sem("rot_ready")
        qkT_psum = sem("qkT_psum")
        qkT_hi_done = sem("qkT_hi_done")
        qkT_lo_done = sem("qkT_lo_done")
        q1T_done = sem("q1T_done")
        k1T_done = sem("k1T_done")
        v_hi_done = sem("v_hi_done")
        v_lo_done = sem("v_lo_done")
        g_ready = sem("g_ready")
        s_psum = sem("s_psum")
        decayed = sem("decayed")
        sT_hi_done = sem("sT_hi_done")
        sT_lo_done = sem("sT_lo_done")
        pv_psum = sem("pv_psum")
        squares = sem("squares")
        gn_eps = sem("gn_eps")
        gn_ready = sem("gn_ready")
        gated_ready = sem("gated_ready")
        chT_psum = sem("chT_psum")
        chT_hi_done = sem("chT_hi_done")
        chT_lo_done = sem("chT_lo_done")
        relu_ready = sem("relu_ready")
        hid_ready = sem("hid_ready")
        q_taken = sem("q_taken")
        k_taken = sem("k_taken")
        dv0_hi_done = sem("dv0_hi_done")
        dv0_lo_done = sem("dv0_lo_done")
        dv1_done = sem("dv1_done")
        rope_step = sem("rope_step")
        q_roped = sem("q_roped")
        k_roped = sem("k_roped")
        dqkT_psum = sem("dqkT_psum")
        dqkT_hi_done = sem("dqkT_hi_done")
        dqkT_lo_done = sem("dqkT_lo_done")
        dq0T_done = sem("dq0T_done")
        dk0T_done = sem("dk0T_done")
        scores_psum = sem("scores_psum")
        masked = sem("masked")
        max_ready = sem("max_ready")
        exp_ready = sem("exp_ready")
        inv_ready = sem("inv_ready")
        probs_ready = sem("probs_ready")
        pT_psum = sem("pT_psum")
        pT_hi_done = sem("pT_hi_done")
        pT_lo_done = sem("pT_lo_done")
        p11T_done = sem("p11T_done")
        o_psum = sem("o_psum")
        oT_hi_done = sem("oT_hi_done")
        oT_lo_done = sem("oT_lo_done")

        def ret_units(h, first=False):
            if first:
                return Unit(RET_BASE + 1), Unit(RET_BASE), Unit(RET_BASE + 2), None
            return tuple(Unit(RET_BASE - 1 + n, 4, h, blocks=(2, 1, 1, 1)[n]) for n in range(4))

        ret_last_out = Unit(RET_BASE + RET_UNITS - 1)

        def mlp_units(m, i, first=False):
            if first:
                return Unit(MLP_BASE[m]), None
            return Unit(MLP_BASE[m] - 1, 2, i), Unit(MLP_BASE[m], 2, i)

        def mlp_last_down(m):
            return Unit(MLP_BASE[m] + MLP_UNITS - 1)

        def dil_units(pair, odd):
            return tuple(Unit(DIL_BASE + 3 * odd + n, 6, pair, DIL_UNIT, NG) for n in range(3))

        def next_dil_unit(pair, odd):
            return Unit(DIL_BASE + 3 * odd + 3, 6, pair, DIL_UNIT, NG)

        dil_out_units = [Unit(DIL_BASE + 3 * HEADS), Unit(DIL_BASE + 3 * HEADS + 1)]

        DIL_PAIRS = HEADS // 2

        block = ctx.enter_context(nc.Block())

        @block.sync
        def _(sp):
            def load(unit, source, wait=True):
                if wait:
                    sp.wait_ge(lo_done, 2 * (unit.number - 1))
                pieces = NG if unit.blocks == NG else 2
                part = unit.size // pieces
                for f in range(pieces):
                    src = source(f)
                    dst = raw[:, unit.slot, f * part:(f + 1) * part].rearrange("p (k c) -> p k c", k=src.shape[1])
                    done = dil_landed[unit.slot] if unit.blocks == NG else raw_landed[unit.slot][f]
                    sp.dma_start(dst, src).then_inc(done, 16)

            w_in = ret_w_in[0].rearrange("(k p) n -> p k n", p=P)

            def qk_cols(h):
                return lambda f: w_in[:, :, bass.ds(f * D_MODEL + h * RET_QK, RET_QK)]

            def v_cols(h):
                return lambda f: w_in[:, 4 * f:4 * f + 4, bass.ds(2 * D_MODEL + h * RET_V, RET_V)]

            def g_cols(h):
                return lambda f: w_in[:, 4 * f:4 * f + 4, bass.ds(4 * D_MODEL + h * RET_V, RET_V)]

            def out_rows(w, i):
                def rows(f):
                    r = w[bass.ds(i * CH + f * (CH // 2), CH // 2), :]
                    return r.rearrange("(k p) n -> p k n", p=P)
                return rows

            x_v = x[0].rearrange("(t p) c -> p t c", p=P)
            qk, v, g, _none = ret_units(0, first=True)

            def load_first_piece(i):
                k0, k1 = FIRST_PIECES[i]
                sp.dma_start(raw[:, v.slot, k0 * CH:k1 * CH].rearrange("p (k c) -> p k c", k=k1 - k0),
                             w_in[:, k0:k1, 2 * D_MODEL:2 * D_MODEL + RET_V]).then_inc(first_landed[i], 16)

            sp.dma_start(ident[:], ident_d).then_inc(ident_landed, 16)
            sp.dma_start(x_res[:, 0, :], x_v[:, 0, :]).then_inc(x_landed[0], 16)
            load_first_piece(0)
            load_first_piece(1)
            sp.dma_start(x_res[:, 1, :], x_v[:, 1, :]).then_inc(x_landed[1], 16)
            for i in range(2, len(FIRST_PIECES)):
                load_first_piece(i)
            for f in range(2):
                rows = slice(4 * f, 4 * f + 4)
                dst = raw[:, qk.slot, f * (UNIT // 2):(f + 1) * (UNIT // 2)].rearrange("p (k c) -> p k c", k=4)
                for n in range(2):
                    sp.dma_start(dst[:, :, n * RET_QK:(n + 1) * RET_QK],
                                 w_in[:, rows, n * D_MODEL:n * D_MODEL + RET_QK]).then_inc(second_landed[f], 16)
            sp.dma_start(ret_rot[:], ret_rot_d).then_inc(tables_landed, 16)
            sp.dma_start(decay[:], decay_d.rearrange("p h c -> p (h c)")).then_inc(tables_landed, 16)
            load(g, g_cols(0))

            def load_ln(n):
                if n:
                    sp.wait_ge(x_ready, 2 * TILES * n)
                for i, w in enumerate((ln_g, ln_b)):
                    sp.dma_start(ln_gb[:, i, :], w[n // 2, n % 2:n % 2 + 1, :].partition_broadcast(P))\
                        .then_inc(ln_landed, 16)

            load_ln(0)
            with sp.Fori(1, RET_HEADS) as h:
                qk, v, g, o = ret_units(h)
                load(qk, qk_cols(h))
                load(v, v_cols(h))
                load(g, g_cols(h))
                load(o, out_rows(ret_w_out[0], h - 1))
            load(ret_last_out, out_rows(ret_w_out[0], RET_HEADS - 1))

            def mlp(m):
                w_up = mlp_w_up[m].rearrange("(k p) n -> p k n", p=P)

                def up_cols(i):
                    return lambda f: w_up[:, 4 * f:4 * f + 4, bass.ds(i * CH, CH)]

                up, _none = mlp_units(m, 0, first=True)
                load(up, up_cols(0))
                with sp.Fori(1, 4) as i:
                    up, down = mlp_units(m, i)
                    load(up, up_cols(i))
                    load(down, out_rows(mlp_w_down[m], i - 1))
                load_ln(2 * m + 1)
                with sp.Fori(4, FF_CHUNKS) as i:
                    up, down = mlp_units(m, i)
                    load(up, up_cols(i))
                    load(down, out_rows(mlp_w_down[m], i - 1))
                load(mlp_last_down(m), out_rows(mlp_w_down[m], FF_CHUNKS - 1))

            mlp(0)

            sp.dma_start(dil_rot[:], dil_rot_d).then_inc(tables_landed, 16)
            sp.wait_ge(sT_lo_done, RET_HEADS)
            sp.dma_start(mask, mask_d).then_inc(tables_landed, 16)
            w_q = dil_w_q[0].rearrange("(k p) n -> p k n", p=P)
            w_kv = kv_w.rearrange("(k p) n -> p k n", p=P)

            def head_cols(w, first, h):
                return lambda g: w[:, :, bass.ds((first + g) * D_MODEL + h * HD, HD)]

            def dil_pair(pair):
                for odd in range(2):
                    h = 2 * pair + odd
                    q, k, v = dil_units(pair, odd)
                    load(q, head_cols(w_q, 0, h))
                    load(k, head_cols(w_kv, 0, h))
                    load(v, head_cols(w_kv, NG, h))

            with sp.Fori(0, DIL_PAIRS) as pair:
                dil_pair(pair)
            load_ln(2)
            w_o = dil_w_out[0].rearrange("(k p) n -> p k n", p=P)
            for n in range(2):
                load(dil_out_units[n], lambda f, n=n: w_o[:, 4 * f:4 * f + 4, n * CH:(n + 1) * CH])

            mlp(1)

            out_v = out[0].rearrange("(t p) c -> p t c", p=P)
            for t in range(TILES):
                for c in range(2):
                    cols = slice(c * CH, (c + 1) * CH)
                    sp.wait_ge(x_ready, 2 * (3 * TILES + t) + c + 1)
                    sp.dma_start(out_v[:, t, cols], x_res[:, t, cols]).then_inc(out_landed, 16)
            sp.wait_ge(out_landed, 16 * 2 * TILES)

        @block.gpsimd
        def _(pool):
            pool.memset(neg_half, -0.5).then_inc(const_done, 1)
            pool.memset(neg_half2, -0.5).then_inc(const_done, 1)
            pool.memset(gn_eps_c, GN_EPS).then_inc(const_done, 1)
            pool.memset(zeros[:], 0.0).then_inc(const_done, 1)
            pool.wait_ge(const_done, 3)

            def group_norm(h):
                pool.wait_ge(squares, TILES * (h + 1))
                pool.tensor_tensor(ms_eps, mean_sq, gn_eps_c, ALU.add).then_inc(gn_eps, 1)
                pool.wait_ge(gn_eps, h + 1)
                pool.tensor_tensor(gn_rstd, ms_eps, neg_half2, ALU.pow).then_inc(gn_ready, 1)

            def eighths(unit, pieces, quarters=None):
                for f in pieces:
                    cols = slice(f * unit.size // 8, (f + 1) * unit.size // 8)
                    if quarters and f == pieces[-1]:
                        pool.wait_ge(quarter_lo, quarters)
                    ins = pool.tensor_tensor(w_lo[:, unit.slot, cols], raw[:, unit.slot, cols],
                                             w_hi[:, unit.slot, cols].bitcast(F32), ALU.subtract)
                if quarters is not None:
                    ins.then_inc(lo_done, 1)

            def layer_norm(n, unit):
                for t in range(TILES):
                    if unit is not None and t == 0:
                        pool.wait_ge(hi_done, 2 * unit.number + 1)
                        eighths(unit, (2, 3), quarters=n + 1)
                    if unit is not None and t == (n == 2):
                        pool.wait_ge(hi_done, 2 * unit.number + 2)
                        eighths(unit, (4, 5))
                    if unit is not None and t == 1:
                        eighths(unit, (6, 7), quarters=0)
                    c = TILES * n + t + 1
                    pool.wait_ge(ln_moments, c)
                    pool.tensor_scalar(var_eps[t], moments[:, t, 1:2], LN_EPS, None, ALU.add).then_inc(ln_eps, 1)
                    pool.wait_ge(ln_eps, c)
                    pool.tensor_tensor(rstd[t], var_eps[t], neg_half, ALU.pow).then_inc(ln_rstd, 1)

            group_norm(0)
            with pool.Fori(1, RET_HEADS) as h:
                group_norm(h)
            for n, unit in enumerate((mlp_units(0, 0, first=True)[0], dil_units(0, 0)[0],
                                      mlp_units(1, 0, first=True)[0], None)):
                if n == 2:
                    o1 = dil_out_units[1]
                    pool.wait_ge(hi_done, 2 * o1.number + 1)
                    pool.wait_ge(lo_done, 2 * o1.number)
                    eighths(o1, (0, 1, 2, 3), quarters=0)
                layer_norm(n, unit)

        @block.scalar
        def _(act):
            def split_hi(unit, wait=True):
                half = unit.size // 2
                for f in range(2):
                    if isinstance(unit.number, int) and unit.number == 1:
                        act.wait_ge(second_landed[f], 16 * 2)
                    elif unit.blocks != NG:
                        act.wait_ge(raw_landed[unit.slot][f], 16 * (unit.turn + 1))
                    elif f == 0:
                        act.wait_ge(dil_landed[unit.slot], 16 * NG * (unit.turn + 1))
                    if wait and f == 0:
                        act.wait_ge(tile_done, 2 * (unit.number - 1))
                    act.activation(w_hi[:, unit.slot, f * half:(f + 1) * half],
                                   raw[:, unit.slot, f * half:(f + 1) * half], ACT.Copy).then_inc(hi_done, 1)

            def take_xT(n, t):
                for b in range(2):
                    act.wait_ge(xT_psum, 2 * (TILES * n + t) + b + 1)
                    act.activation(xT_hi[:, 4 * b:4 * b + 4, t * P:(t + 1) * P],
                                   ps_t[:, b, :].rearrange("p (k c) -> p k c", k=4), ACT.Copy).then_inc(xT_hi_done, 1)

            def take_chT(n, place=0):
                for b in range(2):
                    act.wait_ge(chT_psum, 2 * n + b + 1)
                    act.activation(oT_hi[:, place * CK + 2 * b:place * CK + 2 * b + 2, :],
                                   ps_t[:, b, :].rearrange("p (k c) -> p k c", k=2), ACT.Copy).then_inc(chT_hi_done, 1)

            def head_squares(h):
                act.wait_ge(pv_psum, h + 1)
                for t in range(TILES):
                    act.activation(gated[:, t, :], ps_t[:, t, :], ACT.Square,
                                   scale=RET_V ** -0.5, accum_out=mean_sq[:, t:t + 1])\
                        .then_inc(squares, 1)

            def take_v(v, h):
                for t in range(TILES):
                    act.wait_ge(tile_done, 2 * v.number + t + 1)
                    act.activation(v_hi[:, t, :], ps_proj[:, t, :], ACT.Copy).then_inc(v_hi_done, 1)

            def take_qk(h):
                act.wait_ge(qkT_psum, h + 1)
                q, k = [ps_t[:, s, :].rearrange("p (e n) -> p e n", e=2) for s in range(2)]
                act.activation(q1T, q[:, :, P:SEQ], ACT.Copy).then_inc(q1T_done, 1)
                act.activation(qT_hi, q, ACT.Copy).then_inc(qkT_hi_done, 1)
                act.wait_ge(k1T_done, h + 1)
                act.activation(k0T_hi, k[:, :, 0:P], ACT.Copy).then_inc(qkT_hi_done, 1)

            def take_scores(h):
                act.wait_ge(decayed, h + 1)
                act.activation(sT_hi, sT, ACT.Copy).then_inc(sT_hi_done, 1)

            def silu(g, t):
                act.wait_ge(tile_done, 2 * g.number + t + 1)
                act.activation(silu_g[:, t, :], ps_proj[:, t, :], ACT.Silu).then_inc(g_ready, 1)

            def ret_head(h, last=False):
                qk, v, g, o = ret_units(h)
                head_squares(h - 1)
                split_hi(v)
                take_chT(h - 1)
                split_hi(g)
                take_v(v, h)
                take_qk(h)
                split_hi(o)
                silu(g, 0)
                take_scores(h)
                silu(g, 1)
                if last:
                    head_squares(h)
                split_hi(Unit(RET_BASE + 3, 4, h))

            qk, v, g, _none = ret_units(0, first=True)
            for i, (k0, k1) in enumerate(FIRST_PIECES):
                cols = slice(k0 * CH, k1 * CH)
                act.wait_ge(first_landed[i], 16)
                act.activation(w_hi[:, v.slot, cols], raw[:, v.slot, cols], ACT.Copy)\
                    .then_inc(piece_count(i, first_hi, hi_done)[0], 1)
                if i < TILES:
                    take_xT(0, i)
            split_hi(qk, wait=False)
            take_v(v, 0)
            split_hi(g)
            split_hi(ret_units(1)[0])
            take_qk(0)
            silu(g, 0)
            take_scores(0)
            silu(g, 1)
            with act.Fori(1, RET_HEADS - 1) as h:
                ret_head(h)
            ret_head(RET_HEADS - 1, last=True)
            take_chT(RET_HEADS - 1, place=1)

            def mlp(m):
                up, _none = mlp_units(m, 0, first=True)
                split_hi(up)
                take_xT(2 * m + 1, 0)
                split_hi(mlp_units(m, 1)[0])
                take_xT(2 * m + 1, 1)

                def relu(up, t):
                    act.wait_ge(tile_done, 2 * up.number + t + 1)
                    act.activation(hid[:, t, :], ps_proj[:, t, :], ACT.Relu).then_inc(relu_ready, 1)

                for t in range(TILES):
                    relu(up, t)
                chunk0 = RET_HEADS + m * FF_CHUNKS

                def chunk(i, last=False):
                    up, down = mlp_units(m, i)
                    split_hi(down)
                    take_chT(chunk0 + i - 1)
                    relu(up, 0)
                    relu(up, 1)
                    split_hi(Unit(MLP_BASE[m] + 1, 2, i))

                with act.Fori(1, FF_CHUNKS - 1) as i:
                    chunk(i)
                chunk(FF_CHUNKS - 1)
                take_chT(chunk0 + FF_CHUNKS - 1, place=1)

            mlp(0)

            split_hi(dil_units(0, 0)[0])
            take_xT(2, 0)

            def copy_proj(unit, t, dst, done):
                act.wait_ge(tile_done, 2 * unit.number + t + 1)
                act.activation(dst, ps_proj[:, t, 0:DIL_COLS].rearrange("p (g c) -> p g c", g=NG), ACT.Copy)\
                    .then_inc(done, 1)

            def take_qkT(p):
                act.wait_ge(dqkT_psum, p + 1)
                _q0, q1, k0, k1 = [ps_acc[:, b, 0:NG * P].rearrange("p (g n) -> p g n", g=NG) for b in range(4)]
                act.activation(dq1T_hi, q1, ACT.Copy).then_inc(dqkT_hi_done, 1)
                act.activation(dk0T, k0, ACT.Copy).then_inc(dk0T_done, 1)
                act.activation(dkT_hi[:, :, 0:P], k0, ACT.Copy).then_inc(dqkT_hi_done, 1)
                act.activation(dkT_hi[:, :, P:SEQ], k1, ACT.Copy).then_inc(dqkT_hi_done, 1)

            def softmax_exp(p):
                for t, pt in ((0, p0), (1, p1)):
                    act.wait_ge(max_ready, TILES * p + t + 1)
                    act.activation(pt, pt, ACT.Exp, bias=neg_max[t], scale=DIL_SCALE, accum_out=row_sum[t])\
                        .then_inc(exp_ready, 1)

            def take_pT(p):
                act.wait_ge(pT_psum, p + 1)
                act.activation(pT_hi[:, 0:2], pT_bank(0), ACT.Copy).then_inc(pT_hi_done, 1)
                act.activation(pT_hi[:, 2:3], pT_bank(1), ACT.Copy).then_inc(pT_hi_done, 1)

            def take_oT(p):
                act.wait_ge(o_psum, p + 1)
                act.activation(oT_hi[:].rearrange("p h n -> p (h n)")[:, bass.ds(p * SEQ, SEQ)],
                               ps_acc[:, 0, 0:SEQ], ACT.Copy).then_inc(oT_hi_done, 1)

            def dil_head(pair, odd, first=False, last=False):
                h = 2 * pair + odd
                q, k, v = dil_units(pair, odd)
                if not first:
                    take_qkT(h - 1)
                split_hi(k)
                if first:
                    take_xT(2, 1)
                copy_proj(q, 0, q_nat[:, 0], q_taken)
                if not first:
                    softmax_exp(h - 1)
                copy_proj(q, 1, q_nat[:, 1], q_taken)
                split_hi(v)
                if not first:
                    take_pT(h - 1)
                copy_proj(k, 0, k_nat[:, 0], k_taken)
                copy_proj(k, 1, k_nat[:, 1], k_taken)
                if not first:
                    take_oT(h - 1)
                if last:
                    split_hi(dil_out_units[0])
                else:
                    split_hi(next_dil_unit(pair, odd))
                copy_proj(v, 0, dv0_hi, dv0_hi_done)
                copy_proj(v, 1, dv1, dv1_done)

            dil_head(0, 0, first=True)
            with act.Fori(0, DIL_PAIRS - 1) as pair:
                dil_head(pair, 1)
                dil_head(pair + 1, 0)
            dil_head(DIL_PAIRS - 1, 1, last=True)
            take_qkT(HEADS - 1)
            split_hi(dil_out_units[1])
            softmax_exp(HEADS - 1)
            take_pT(HEADS - 1)
            take_oT(HEADS - 1)

            mlp(1)

        @block.vector
        def _(dve):
            def split_lo(unit, halves=(0, 1)):
                half = unit.size // 2
                for f in halves:
                    cols = slice(f * half, (f + 1) * half)
                    dve.wait_ge(hi_done, 2 * unit.number + f + 1)
                    dve.tensor_tensor(w_lo[:, unit.slot, cols], raw[:, unit.slot, cols],
                                      w_hi[:, unit.slot, cols].bitcast(F32), ALU.subtract).then_inc(lo_done, 1)

            def take_xT(n, t, halves=(0, 1)):
                for b in halves:
                    dve.wait_ge(xT_hi_done, 2 * TILES * n + 2 * t + b + 1)
                    s = slice(t * P, (t + 1) * P)
                    dve.tensor_tensor(xT_lo[:, 4 * b:4 * b + 4, s], ps_t[:, b, :].rearrange("p (k c) -> p k c", k=4),
                                      xT_hi[:, 4 * b:4 * b + 4, s].bitcast(F32), ALU.subtract).then_inc(xT_lo_done, 1)

            def take_chT(n, place=0):
                for b in range(2):
                    ks = slice(place * CK + 2 * b, place * CK + 2 * b + 2)
                    dve.wait_ge(chT_hi_done, 2 * n + b + 1)
                    dve.tensor_tensor(oT_lo[:, ks, :], ps_t[:, b, :].rearrange("p (k c) -> p k c", k=2),
                                      oT_hi[:, ks, :].bitcast(F32), ALU.subtract)\
                        .then_inc(chT_lo_done, 1)

            def nth(n, t, c):
                return 2 * c + t + 1 if n == 2 else 2 * t + c + 1

            def ln_sum(n, t, c, last_unit, src):
                if c == 0 and n != 2:
                    dve.wait_ge(acc_half, TILES * (n - (n > 2)) + t + 1)
                elif c == 0:
                    dve.wait_ge(tile_done, 2 * dil_out_units[0].number + t + 1)
                else:
                    dve.wait_ge(tile_done, 2 * last_unit.number + t + 1)
                half = x_res[:, t, c * CH:(c + 1) * CH]
                dve.scalar_tensor_tensor(out=half, in0=half, scalar=ALPHA, in1=src(t, c), op0=ALU.mult, op1=ALU.add)\
                    .then_inc(ln_summed, 1)

            def ln_stats(n, t, c):
                dve.wait_ge(ln_summed, 2 * TILES * n + nth(n, t, c))
                dve.bn_stats(stats[:, t, c, :], x_res[:, t, c * CH:(c + 1) * CH]).then_inc(ln_counted, 1)

            def ln_rows(n, t):
                dve.wait_ge(ln_counted, 2 * TILES * n + nth(n, t, 1))
                dve.bn_aggr(moments[:, t, :], stats[:, t, :, :]).then_inc(ln_moments, 1)
                dve.wait_ge(ln_moments, TILES * n + t + 1)
                dve.wait_ge(ln_landed, 32 * (n + 1))
                for c in range(2):
                    half = x_res[:, t, c * CH:(c + 1) * CH]
                    dve.scalar_tensor_tensor(out=half, in0=half, scalar=moments[:, t, 0:1],
                                             in1=ln_gb[:, 0, c * CH:(c + 1) * CH], op0=ALU.subtract, op1=ALU.mult)\
                        .then_inc(ln_gained, 1)
                dve.wait_ge(ln_rstd, TILES * n + t + 1)
                for c in range(2):
                    half = x_res[:, t, c * CH:(c + 1) * CH]
                    dve.wait_ge(ln_gained, 2 * (TILES * n + t) + c + 1)
                    dve.scalar_tensor_tensor(out=half, in0=half, scalar=rstd[t], in1=ln_gb[:, 1, c * CH:(c + 1) * CH],
                                             op0=ALU.mult, op1=ALU.add).then_inc(x_ready, 1)

            def rotate(qk, t, h):
                dve.wait_ge(tile_done, 2 * qk.number + t + 1)
                c = TILES * h + t
                pairs = ps_proj[:, t, :].rearrange("p (c e) -> p e c", e=2)
                cos = ret_rot[:, t, 0:1, :].to_broadcast([P, 2, 2 * RET_HALF])
                sin = ret_rot[:, t, 1:2, :].to_broadcast([P, 2, 2 * RET_HALF])
                mc, ms = even_odd(rot_c), even_odd(rot_s)
                dve.tensor_tensor(mc, pairs, cos, ALU.mult).then_inc(rot_step, 1)
                dve.tensor_tensor(ms, pairs, sin, ALU.mult).then_inc(qk_taken, 1)
                dve.wait_ge(rot_step, 2 * c + 1)
                dve.wait_ge(qk_taken, c + 1)
                dve.tensor_tensor(rot[:, t, 0, :], mc[:, 0], ms[:, 1], ALU.subtract).then_inc(rot_step, 1)
                dve.tensor_tensor(rot[:, t, 1, :], mc[:, 1], ms[:, 0], ALU.add).then_inc(rot_ready, 1)
                dve.wait_ge(rot_step, 2 * c + 2)
                dve.wait_ge(rot_ready, c + 1)

            def gate(h):
                dve.wait_ge(gn_ready, h + 1)
                for t in range(TILES):
                    dve.wait_ge(g_ready, TILES * h + t + 1)
                    dve.scalar_tensor_tensor(out=gated[:, t, :], in0=ps_t[:, t, :], scalar=gn_rstd[:, t:t + 1],
                                             in1=silu_g[:, t, :], op0=ALU.mult, op1=ALU.mult)\
                        .then_inc(gated_ready, 1)

            def rest(lo, whole, hi, done):
                dve.tensor_tensor(lo, whole, hi.bitcast(F32), ALU.subtract).then_inc(done, 1)

            def take_v(h):
                for t in range(TILES):
                    dve.wait_ge(v_hi_done, TILES * h + t + 1)
                    rest(v_lo[:, t, :], ps_proj[:, t, :], v_hi[:, t, :], v_lo_done)

            def take_qk(h):
                q, k = [ps_t[:, s, :].rearrange("p (e n) -> p e n", e=2) for s in range(2)]
                dve.wait_ge(qkT_psum, h + 1)
                dve.tensor_copy(k1T, k[:, :, P:SEQ]).then_inc(k1T_done, 1)
                dve.wait_ge(qkT_hi_done, 2 * h + 1)
                rest(qT_lo, q, qT_hi, qkT_lo_done)
                dve.wait_ge(qkT_hi_done, 2 * h + 2)
                rest(k0T_lo, k[:, :, 0:P], k0T_hi, qkT_lo_done)

            def decay_scores(h):
                dve.wait_ge(s_psum, h + 1)
                dve.tensor_tensor(sT, ps_t[:, 0, 0:3 * P], decay[:, bass.ds(h * 3 * P, 3 * P)], ALU.mult)\
                    .then_inc(decayed, 1)

            def take_scores(h):
                dve.wait_ge(sT_hi_done, h + 1)
                rest(sT_lo, sT, sT_hi, sT_lo_done)

            def ret_head(h, last=False):
                qk, v, g, o = ret_units(h)
                gate(h - 1)
                split_lo(v)
                rotate(qk, 0, h)
                rotate(qk, 1, h)
                take_chT(h - 1)
                split_lo(g)
                take_v(h)
                take_qk(h)
                split_lo(o, halves=(0,))
                decay_scores(h)
                split_lo(o, halves=(1,))
                take_scores(h)
                if last:
                    gate(h)
                split_lo(Unit(RET_BASE + 3, 4, h))

            qk, v, g, _none = ret_units(0, first=True)
            for i, (k0, k1) in enumerate(FIRST_PIECES):
                cols = slice(k0 * CH, k1 * CH)
                dve.wait_ge(*piece_count(i, first_hi, hi_done))
                dve.tensor_tensor(w_lo[:, v.slot, cols], raw[:, v.slot, cols], w_hi[:, v.slot, cols].bitcast(F32),
                                  ALU.subtract).then_inc(piece_count(i, first_lo, lo_done)[0], 1)
                if i < TILES:
                    take_xT(0, i)
            split_lo(qk, halves=(0,))
            take_v(0)
            split_lo(qk, halves=(1,))
            dve.wait_ge(tables_landed, 16 * 2)
            split_lo(g, halves=(0,))
            rotate(qk, 0, 0)
            split_lo(g, halves=(1,))
            rotate(qk, 1, 0)
            split_lo(ret_units(1)[0], halves=(0,))
            take_qk(0)
            split_lo(ret_units(1)[0], halves=(1,))
            decay_scores(0)
            take_scores(0)
            with dve.Fori(1, RET_HEADS - 1) as h:
                ret_head(h)
            ret_head(RET_HEADS - 1, last=True)
            take_chT(RET_HEADS - 1, place=1)

            def layer_norm(n, last_unit, src, unit=None):
                early = [(0, 0), (1, 0)] if n == 2 else []
                for t, c in early:
                    ln_sum(n, t, c, last_unit, src)
                    ln_stats(n, t, c)
                if unit is not None:
                    cols = slice(0, unit.size // 4)
                    dve.wait_ge(hi_done, 2 * unit.number + 1)
                    dve.tensor_tensor(w_lo[:, unit.slot, cols], raw[:, unit.slot, cols],
                                      w_hi[:, unit.slot, cols].bitcast(F32), ALU.subtract).then_inc(quarter_lo, 1)
                for c in range(2):
                    if (0, c) not in early:
                        ln_sum(n, 0, c, last_unit, src)
                        ln_stats(n, 0, c)
                ln_rows(n, 0)
                if not early:
                    ln_sum(n, 1, 0, last_unit, src)
                if unit is not None:
                    take_xT(n + 1, 0)
                ln_sum(n, 1, 1, last_unit, src)
                for c in range(2):
                    if (1, c) not in early:
                        ln_stats(n, 1, c)
                ln_rows(n, 1)
                if unit is not None:
                    take_xT(n + 1, 1)
                    dve.wait_ge(lo_done, 2 * unit.number + 2)

            def mlp(m, last_unit, src):
                up, _none = mlp_units(m, 0, first=True)
                layer_norm(2 * m, last_unit, src, up)

                def square(t, n):
                    dve.wait_ge(relu_ready, TILES * n + t + 1)
                    dve.tensor_tensor(hid_sq[:, t, :], hid[:, t, :], hid[:, t, :], ALU.mult).then_inc(hid_ready, 1)

                n0 = m * FF_CHUNKS
                split_lo(mlp_units(m, 1)[0])
                square(0, n0)
                square(1, n0)

                def chunk(i):
                    up, down = mlp_units(m, i)
                    split_lo(down)
                    take_chT(RET_HEADS + n0 + i - 1)
                    square(0, n0 + i)
                    square(1, n0 + i)
                    split_lo(Unit(MLP_BASE[m] + 1, 2, i))

                with dve.Fori(1, FF_CHUNKS - 1) as i:
                    chunk(i)
                chunk(FF_CHUNKS - 1)
                take_chT(RET_HEADS + n0 + FF_CHUNKS - 1, place=1)

            mlp(0, ret_last_out, acc)

            layer_norm(1, mlp_last_down(0), acc, dil_units(0, 0)[0])
            dve.wait_ge(tables_landed, 16 * 4)

            def rope(nat, h, is_k, roped):
                n = 2 * h + is_k
                x12 = nat[:, :, :, 0:ROT]
                cos = dil_rot[:, :, 0:1, :].to_broadcast([P, TILES, NG, ROT])
                sin = dil_rot[:, :, 1:2, :].to_broadcast([P, TILES, NG, ROT])
                hr = ROT // 2
                dve.tensor_tensor(dil_c, x12, cos, ALU.mult).then_inc(rope_step, 1)
                dve.tensor_tensor(dil_s, x12, sin, ALU.mult).then_inc(rope_step, 1)
                dve.wait_ge(rope_step, 3 * n + 2)
                dve.tensor_tensor(nat[:, :, :, 0:hr], dil_c[:, :, :, 0:hr], dil_s[:, :, :, hr:ROT], ALU.subtract)\
                    .then_inc(rope_step, 1)
                dve.tensor_tensor(nat[:, :, :, hr:ROT], dil_c[:, :, :, hr:ROT], dil_s[:, :, :, 0:hr], ALU.add)\
                    .then_inc(roped, 1)
                dve.wait_ge(rope_step, 3 * n + 3)
                dve.wait_ge(roped, h + 1)

            def take_qkT(p):
                dve.wait_ge(dqkT_psum, p + 1)
                q0, q1, k0, k1 = [ps_acc[:, b, 0:NG * P].rearrange("p (g n) -> p g n", g=NG) for b in range(4)]
                dve.tensor_copy(dq0T, q0).then_inc(dq0T_done, 1)
                for n, (lo, whole, hi) in enumerate(((dq1T_lo, q1, dq1T_hi),
                                                     (dkT_lo[:, :, 0:P], k0, dkT_hi[:, :, 0:P]),
                                                     (dkT_lo[:, :, P:SEQ], k1, dkT_hi[:, :, P:SEQ]))):
                    dve.wait_ge(dqkT_hi_done, 3 * p + n + 1)
                    rest(lo, whole, hi, dqkT_lo_done)

            def take_dv0(h):
                dve.wait_ge(dv0_hi_done, h + 1)
                rest(dv0_lo, ps_proj[:, 0, 0:DIL_COLS].rearrange("p (g c) -> p g c", g=NG), dv0_hi, dv0_lo_done)

            def softmax_max(p):
                parts = ((0, p0, ps_acc[:, 0, 0:S0], mask[:, 0:S0]),
                         (1, p1, ps_t[:].rearrange("p b n -> p (b n)")[:, 0:S1], mask[:, S0:]))
                for t, pt, scores, m in parts:
                    dve.wait_ge(scores_psum, TILES * p + t + 1)
                    dve.memset(wait_cell[t], 0.0)
                    dve.tensor_tensor_reduce(pt, scores, m, 1.0, -3.0e38, ALU.add, ALU.max, row_max[t])\
                        .then_inc(masked, 1)
                    dve.wait_ge(masked, TILES * p + t + 1)
                    dve.tensor_scalar(neg_max[t], row_max[t], -DIL_SCALE, None, ALU.mult).then_inc(max_ready, 1)

            def softmax_norm(p):
                for t, pt in ((0, p0), (1, p1)):
                    dve.wait_ge(exp_ready, TILES * p + t + 1)
                    dve.reciprocal(row_inv[t], row_sum[t]).then_inc(inv_ready, 1)
                    dve.wait_ge(inv_ready, TILES * p + t + 1)
                    dve.tensor_scalar(pt, pt, row_inv[t], None, ALU.mult).then_inc(probs_ready, 1)

            def take_pT(p):
                dve.wait_ge(pT_psum, p + 1)
                dve.tensor_copy(p11T, ps_acc[:, 3, 0:NG * P].rearrange("p (g n) -> p g n", g=NG))\
                    .then_inc(p11T_done, 1)
                for b, gs in enumerate((slice(0, 2), slice(2, 3))):
                    dve.wait_ge(pT_hi_done, 2 * p + b + 1)
                    rest(pT_lo[:, gs], pT_bank(b), pT_hi[:, gs], pT_lo_done)

            def take_oT(p):
                dve.wait_ge(oT_hi_done, p + 1)
                cols = bass.ds(p * SEQ, SEQ)
                dve.tensor_tensor(oT_lo[:].rearrange("p h n -> p (h n)")[:, cols], ps_acc[:, 0, 0:SEQ],
                                  oT_hi[:].rearrange("p h n -> p (h n)")[:, cols].bitcast(F32), ALU.subtract)\
                    .then_inc(oT_lo_done, 1)

            def dil_head(pair, odd, first=False, last=False):
                h = 2 * pair + odd
                q, k, v = dil_units(pair, odd)
                if not first:
                    take_qkT(h - 1)
                split_lo(k, halves=(0,))
                if not first:
                    softmax_max(h - 1)
                split_lo(k, halves=(1,))
                if not first:
                    softmax_norm(h - 1)
                dve.wait_ge(q_taken, TILES * (h + 1))
                rope(q_nat, h, 0, q_roped)
                split_lo(v)
                if not first:
                    take_pT(h - 1)
                dve.wait_ge(k_taken, TILES * (h + 1))
                rope(k_nat, h, 1, k_roped)
                if not first:
                    take_oT(h - 1)
                if last:
                    split_lo(dil_out_units[0])
                else:
                    split_lo(next_dil_unit(pair, odd))
                take_dv0(h)

            dil_head(0, 0, first=True)
            with dve.Fori(0, DIL_PAIRS - 1) as pair:
                dil_head(pair, 1)
                dil_head(pair + 1, 0)
            dil_head(DIL_PAIRS - 1, 1, last=True)
            take_qkT(HEADS - 1)
            softmax_max(HEADS - 1)
            softmax_norm(HEADS - 1)
            take_pT(HEADS - 1)
            dve.wait_ge(lo_done, 2 * dil_out_units[1].number + 1)
            split_lo(dil_out_units[1], halves=(1,))
            take_oT(HEADS - 1)

            mlp(1, dil_out_units[1], dil_out)
            layer_norm(2 * DEPTH - 1, mlp_last_down(1), acc)

        @block.tensor
        def _(pe):
            def product(dst, hi, lo, whi, wlo, start, stop, **kw):
                pe.matmul(dst, hi, whi, start=start, stop=False, **kw)
                pe.matmul(dst, hi, wlo, start=False, stop=False, **kw)
                return pe.matmul(dst, lo, whi, start=False, stop=stop, **kw)

            def open_accumulators(banks):
                for bank in banks:
                    pe.matmul(bank, zeros[:, 0:P], zeros[:], start=True, stop=False)

            def keep_clock(count):
                for _n in range(count):
                    pe.matmul(acc(0, 0), zeros[:, 0:P], zeros[:], start=False, stop=False)

            def wide(unit, t, ks, xh, xl, dst, cols, wait=True, done=tile_done, new_x=None):
                half = KT // 2

                def tile(w, k):
                    if unit.blocks == 1:
                        return w[:, unit.slot, k * cols:(k + 1) * cols]
                    blocks = w[:, unit.slot, 0:unit.size].rearrange("p (b k c) -> p k b c", b=unit.blocks, k=KT)
                    return blocks[:, k]

                for k in ks:
                    if wait and unit.blocks == 1 and k % half == 0:
                        pe.wait_ge(lo_done, 2 * unit.number + k // half + 1)
                    elif wait and k == 0:
                        pe.wait_ge(lo_done, 2 * unit.number + 2)
                    if new_x is not None and k % half == 0:
                        pe.wait_ge(xT_lo_done, 2 * (TILES * new_x + t) + k // half + 1)
                    x_ = slice(t * P, (t + 1) * P)
                    last = product(dst, xh[:, k, x_], xl[:, k, x_], tile(w_hi, k), tile(w_lo, k),
                                   start=(k == 0), stop=(k == KT - 1))
                if done is not None:
                    last.then_inc(done, 1)

            def project(unit, t, cols, new_x=None, ks=range(KT)):
                wide(unit, t, ks, xT_hi, xT_lo, ps_proj[:, t, 0:cols], cols, wait=(t == 0),
                     done=tile_done if ks[-1] == KT - 1 else None, new_x=new_x)

            def accumulate(unit, t, place=0, last_of_stage=False, new_x=None):
                order = [(k, n) for k in range(CK) for n in range(2)]
                if last_of_stage:
                    order.sort(key=lambda kn: kn[1])
                for k, n in order:
                    if new_x is not None and n == 1 and k >= CK - 2:
                        transpose_x(new_x, 0, halves=(k - (CK - 2),))
                    if t == 0 and n == 0 and k % 2 == 0:
                        pe.wait_ge(lo_done, 2 * unit.number + k // 2 + 1)
                    w = slice(k * D_MODEL + n * CH, k * D_MODEL + (n + 1) * CH)
                    x_ = slice(t * P, (t + 1) * P)
                    last = product(acc(t, n), oT_hi[:, place * CK + k, x_], oT_lo[:, place * CK + k, x_],
                                   w_hi[:, unit.slot, w], w_lo[:, unit.slot, w],
                                   start=False, stop=(last_of_stage and k == CK - 1))
                    if last_of_stage and (k, n) == (CK - 1, 0):
                        last.then_inc(acc_half, 1)
                last.then_inc(tile_done, 1)

            def transpose_x(n, t, halves=(0, 1)):
                for b in halves:
                    if n:
                        pe.wait_ge(x_ready, 2 * (TILES * (n - 1) + t) + b + 1)
                    if t:
                        pe.wait_ge(xT_lo_done, 2 * TILES * n + b + 1)
                    for k in range(4):
                        c = (4 * b + k) * P
                        last = pe.transpose(ps_t[:, b, k * P:(k + 1) * P], x_res[:, t, c:c + P], ident[:])
                    last.then_inc(xT_psum, 1)

            def transpose_chunk(src):
                for k in range(CK):
                    for t in range(TILES):
                        c = (k % 2) * SEQ + t * P
                        last = pe.transpose(ps_t[:, k // 2, c:c + P], src[:, t, k * P:(k + 1) * P], ident[:])
                    if k % 2 == 1:
                        last.then_inc(chT_psum, 1)

            pe.wait_ge(const_done, 4)
            open_accumulators([acc(t, n) for t in range(TILES) for n in range(2)])
            keep_clock(4)
            pe.wait_ge(ident_landed, 16)
            pe.wait_ge(x_landed[0], 16)
            transpose_x(0, 0)
            keep_clock(3)

            def transpose_gated(h):
                pe.wait_ge(gated_ready, TILES * (h + 1))
                transpose_chunk(gated)

            def project_taken(unit, taken, h):
                for t in range(TILES):
                    pe.wait_ge(taken, TILES * h + t + 1)
                    project(unit, t, CH)

            def transpose_rotated():
                for s in range(2):
                    for e in range(2):
                        for t in range(TILES):
                            last = pe.transpose(ps_t[:, s, e * SEQ + t * P:e * SEQ + (t + 1) * P],
                                                rot[:, t, e, s * RET_HALF:(s + 1) * RET_HALF], ident[:])
                last.then_inc(qkT_psum, 1)

            def ret_scores(h):
                pe.wait_ge(qkT_lo_done, 2 * (h + 1))
                for e in range(2):
                    product(ps_t[:, 0, 0:SEQ], k0T_hi[:, e], k0T_lo[:, e], qT_hi[:, e], qT_lo[:, e],
                            start=(e == 0), stop=(e == 1))
                pe.wait_ge(q1T_done, h + 1)
                pe.wait_ge(k1T_done, h + 1)
                for e in range(2):
                    last = pe.matmul(ps_t[:, 0, SEQ:SEQ + P], k1T[:, e], q1T[:, e], start=(e == 0), stop=(e == 1))
                last.then_inc(s_psum, 1)

            def gate_and_scores(g, h):
                pe.wait_ge(v_lo_done, TILES * h + 1)
                project(g, 0, CH)
                ret_scores(h)
                pe.wait_ge(v_lo_done, TILES * h + 2)
                project(g, 1, CH)

            def ret_values(h):
                pe.wait_ge(sT_lo_done, h + 1)
                for block, t, keys in ((0, 0, 0), (1, 1, 0), (2, 1, 1)):
                    s_ = slice(block * P, (block + 1) * P)
                    last = product(ps_t[:, t, :], sT_hi[:, s_], sT_lo[:, s_], v_hi[:, keys, :], v_lo[:, keys, :],
                                   start=(keys == 0), stop=(keys == t))
                last.then_inc(pv_psum, 1)

            def ret_head(h, last=False):
                qk, v, g, o = ret_units(h)
                project_taken(qk, g_ready, h - 1)
                transpose_gated(h - 1)
                project_taken(v, qk_taken, h)
                pe.wait_ge(rot_ready, TILES * (h + 1))
                pe.wait_ge(chT_lo_done, 2 * h)
                transpose_rotated()
                gate_and_scores(g, h)
                if last:
                    ret_values(h)
                    accumulate(o, 0)
                    transpose_gated(h)
                    accumulate(o, 1)
                else:
                    accumulate(o, 0)
                    accumulate(o, 1)
                    ret_values(h)

            qk, v, g, _none = ret_units(0, first=True)
            def first_piece(i, t):
                wide(v, t, range(*FIRST_PIECES[i]), xT_hi, xT_lo, ps_proj[:, t, :], CH, wait=False,
                     done=tile_done if i == len(FIRST_PIECES) - 1 else None, new_x=0)

            for i in range(2):
                pe.wait_ge(*piece_count(i, first_lo, lo_done))
                first_piece(i, 0)
                if i == 0:
                    pe.wait_ge(x_landed[1], 16)
                    transpose_x(0, 1)
            for i in range(2):
                first_piece(i, 1)
            for i in range(2, len(FIRST_PIECES)):
                pe.wait_ge(*piece_count(i, first_lo, lo_done))
                for t in range(TILES):
                    first_piece(i, t)
            project_taken(qk, v_lo_done, 0)
            pe.wait_ge(qk_taken, 1)
            project(g, 0, CH)
            pe.wait_ge(rot_ready, TILES)
            transpose_rotated()
            pe.wait_ge(qk_taken, 2)
            project(g, 1, CH, ks=range(KT // 2))
            ret_scores(0)
            project(g, 1, CH, ks=range(KT // 2, KT))
            ret_values(0)
            with pe.Fori(1, RET_HEADS - 1) as h:
                ret_head(h)
            ret_head(RET_HEADS - 1, last=True)
            pe.wait_ge(chT_lo_done, 2 * RET_HEADS)
            accumulate(ret_last_out, 0, place=1, last_of_stage=True)
            accumulate(ret_last_out, 1, place=1, last_of_stage=True, new_x=1)

            def first_unit(unit, n, cols, open_acc):
                if open_acc:
                    open_accumulators([acc(0, c) for c in range(2)])
                project(unit, 0, cols, new_x=n, ks=range(KT - 2))
                for b in range(2):
                    transpose_x(n, 1, halves=(b,))
                    project(unit, 0, cols, new_x=n, ks=[KT - 2 + b])
                if open_acc:
                    open_accumulators([acc(1, c) for c in range(2)])
                project(unit, 1, cols, new_x=n)

            def mlp(m):
                up, _none = mlp_units(m, 0, first=True)
                first_unit(up, 2 * m + 1, CH, open_acc=True)
                n0 = m * FF_CHUNKS

                def transpose_hidden(i):
                    pe.wait_ge(hid_ready, TILES * (n0 + i + 1))
                    transpose_chunk(hid_sq)

                def chunk(i, last=False):
                    up, down = mlp_units(m, i)
                    pe.wait_ge(relu_ready, TILES * (n0 + i - 1) + 1)
                    project(up, 0, CH)
                    transpose_hidden(i - 1)
                    project(up, 1, CH)
                    pe.wait_ge(chT_lo_done, 2 * (RET_HEADS + n0 + i))
                    accumulate(down, 0)
                    if last:
                        transpose_hidden(i)
                    accumulate(down, 1)

                with pe.Fori(1, FF_CHUNKS - 1) as i:
                    chunk(i)
                chunk(FF_CHUNKS - 1, last=True)
                pe.wait_ge(chT_lo_done, 2 * (RET_HEADS + n0 + FF_CHUNKS))
                for t in range(TILES):
                    accumulate(mlp_last_down(m), t, place=1, last_of_stage=True,
                               new_x=2 if (m, t) == (0, 1) else None)

            mlp(0)

            def transpose_qk(p):
                pe.wait_ge(q_roped, p + 1)
                pe.wait_ge(k_roped, p + 1)
                for first_bank, nat in ((0, q_nat), (2, k_nat)):
                    for t in range(TILES):
                        for g in range(NG):
                            last = pe.transpose(ps_acc[:, first_bank + t, g * P:(g + 1) * P], nat[:, t, g, :],
                                                ident[:])
                last.then_inc(dqkT_psum, 1)

            def scores(p):
                pe.wait_ge(dq0T_done, p + 1)
                pe.wait_ge(dk0T_done, p + 1)
                for g in range(NG):
                    last = pe.matmul(ps_acc[:, 0, g * P:(g + 1) * P], dq0T[:, g], dk0T[:, g], start=True, stop=True)
                last.then_inc(scores_psum, 1)
                pe.wait_ge(dqkT_lo_done, 3 * (p + 1))
                for g in range(NG):
                    last = product(ps_t[:, g // 2, (g % 2) * SEQ:(g % 2 + 1) * SEQ], dq1T_hi[:, g], dq1T_lo[:, g],
                                   dkT_hi[:, g], dkT_lo[:, g], start=True, stop=True)
                last.then_inc(scores_psum, 1)

            def transpose_probs(p):
                pe.wait_ge(probs_ready, TILES * (p + 1))
                for g in range(NG):
                    for t, part in enumerate((p0[:, g * P:(g + 1) * P], p1[:, g * SEQ:g * SEQ + P])):
                        pe.transpose(pT_bank(g // 2)[:, g % 2, t * P:(t + 1) * P], part, ident[:])
                for g in range(NG):
                    last = pe.transpose(ps_acc[:, 3, g * P:(g + 1) * P], p1[:, g * SEQ + P:(g + 1) * SEQ], ident[:])
                last.then_inc(pT_psum, 1)

            def values(p):
                pe.wait_ge(dv0_lo_done, p + 1)
                for g in range(NG):
                    pe.wait_ge(pT_lo_done, 2 * p + g // 2 + 1)
                    product(ps_acc[:, 0, 0:SEQ], dv0_hi[:, g], dv0_lo[:, g], pT_hi[:, g], pT_lo[:, g],
                            start=(g == 0), stop=(g == NG - 1), skip_group_check=True)
                pe.wait_ge(dv1_done, p + 1)
                pe.wait_ge(p11T_done, p + 1)
                for g in range(NG):
                    last = pe.matmul(ps_acc[:, 0, P:SEQ], dv1[:, g], p11T[:, g], start=False, stop=(g == NG - 1),
                                     skip_group_check=True)
                last.then_inc(o_psum, 1)

            def dil_head(pair, odd, first=False):
                h = 2 * pair + odd
                q, k, v = dil_units(pair, odd)
                if first:
                    first_unit(q, 2, DIL_COLS, open_acc=False)
                else:
                    if not (isinstance(h, int) and h == 1):
                        pe.wait_ge(oT_lo_done, h - 1)
                    transpose_qk(h - 1)
                    pe.wait_ge(dv0_lo_done, h)
                    project(q, 0, DIL_COLS)
                    scores(h - 1)
                    pe.wait_ge(dv1_done, h)
                    project(q, 1, DIL_COLS)
                pe.wait_ge(q_taken, TILES * h + 1)
                project(k, 0, DIL_COLS)
                if not first:
                    transpose_probs(h - 1)
                pe.wait_ge(q_taken, TILES * (h + 1))
                project(k, 1, DIL_COLS)
                if not first:
                    values(h - 1)
                for t in range(TILES):
                    pe.wait_ge(k_taken, TILES * h + t + 1)
                    project(v, t, DIL_COLS)

            dil_head(0, 0, first=True)
            with pe.Fori(0, DIL_PAIRS - 1) as pair:
                dil_head(pair, 1)
                dil_head(pair + 1, 0)
            dil_head(DIL_PAIRS - 1, 1)
            last_h = HEADS - 1
            pe.wait_ge(oT_lo_done, last_h)
            transpose_qk(last_h)
            pe.wait_ge(dv0_lo_done, HEADS)
            o0, o1 = dil_out_units
            wide(o0, 0, range(KT - 3), oT_hi, oT_lo, dil_out(0, 0), CH, done=None)
            scores(last_h)
            pe.wait_ge(dv1_done, HEADS)
            wide(o0, 0, [KT - 3], oT_hi, oT_lo, dil_out(0, 0), CH, wait=False, done=None)
            wide(o0, 1, range(KT - 3), oT_hi, oT_lo, dil_out(1, 0), CH, wait=False, done=None)
            transpose_probs(last_h)
            wide(o0, 0, [KT - 2], oT_hi, oT_lo, dil_out(0, 0), CH, wait=False, done=None)
            wide(o0, 1, range(KT - 3, KT - 1), oT_hi, oT_lo, dil_out(1, 0), CH, wait=False, done=None)
            pe.wait_ge(pT_lo_done, 2 * HEADS)
            wide(o1, 0, range(2), oT_hi, oT_lo, dil_out(0, 1), CH, done=None)
            values(last_h)
            wide(o1, 0, range(2, 4), oT_hi, oT_lo, dil_out(0, 1), CH, done=None)
            pe.wait_ge(oT_lo_done, HEADS)
            wide(o0, 0, [KT - 1], oT_hi, oT_lo, dil_out(0, 0), CH, wait=False)
            wide(o0, 1, [KT - 1], oT_hi, oT_lo, dil_out(1, 0), CH, wait=False)
            wide(o1, 0, range(4, KT), oT_hi, oT_lo, dil_out(0, 1), CH)
            wide(o1, 1, range(KT - 1), oT_hi, oT_lo, dil_out(1, 1), CH, wait=False, done=None)
            transpose_x(3, 0, halves=(0,))
            wide(o1, 1, [KT - 1], oT_hi, oT_lo, dil_out(1, 1), CH, wait=False)
            transpose_x(3, 0, halves=(1,))

            mlp(1)


_INS = ["x", "ret_w_in", "ret_w_out", "kv_w", "dil_w_q", "dil_w_out", "mlp_w_up", "mlp_w_down", "ln_g", "ln_b"]


def kernel(**inputs):
    import concourse.bacc as bacc
    from concourse.bass_utils import run_bass_kernel_spmd

    nc = bacc.Bacc("TRN2", target_bir_lowering=False, num_devices=1)
    arrays = {name: np.ascontiguousarray(inputs[name]) for name in _INS}
    arrays.update({name: np.ascontiguousarray(a) for name, a in stage_tables().items()})
    args = [nc.dram_tensor(f"in_{name}", a.shape, F32, kind="ExternalInput").ap() for name, a in arrays.items()]
    out = nc.dram_tensor("out", (1, SEQ, D_MODEL), F32, kind="ExternalOutput").ap()
    trunk(nc, *args, out)
    r = run_bass_kernel_spmd(nc, [{f"in_{name}": a for name, a in arrays.items()}], core_ids=[0])
    return r.results[0]["out"]
```
